# Optimizing a Trainium2 kernel written in Bass

```python
import math
import jax, jax.numpy as jnp
from jax import lax
import numpy as np

D_MODEL = 1024
BATCH = 1
SEQ = 2048
DEPTH = 1

MIX_WIDTH = D_MODEL
ATTN_WIDTH = MIX_WIDTH // 2
SSM_WIDTH = MIX_WIDTH - ATTN_WIDTH
N_ATTN_HEADS = 4
ATTN_HEAD_DIM = ATTN_WIDTH // (2 * N_ATTN_HEADS)
ATTN_VALUE_DIM = 2 * ATTN_HEAD_DIM
Q_BLOCK = 128
SSM_GROUP = 16
N_SSM_GROUPS = SSM_WIDTH // SSM_GROUP
SSM_STATE = 64
DT_MIN = 1e-3
DT_MAX = 1e-1
N_EXPERT_GROUPS = 4
EXPERTS_PER_GROUP = 8
N_EXPERTS = N_EXPERT_GROUPS * EXPERTS_PER_GROUP
TOP_K_INNER = 2
EXPERT_FF = 512
MOE_BLOCK = 128
IN_COLS = 3 * ATTN_WIDTH + SSM_WIDTH
RMS_EPS = 1e-6

kernel_name = "hymba_diffattn_s5_hiermoe_block"

def rmsnorm(x, gain):
    xf = x.astype(jnp.float32)
    y = xf * lax.rsqrt(jnp.mean(xf * xf, axis=-1, keepdims=True) + RMS_EPS) * gain.astype(jnp.float32)
    return y.astype(x.dtype)

def lambda_init_fn(layer_idx):
    return 0.8 - 0.6 * math.exp(-0.3 * layer_idx)

def alibi_slopes(n_heads):
    return jnp.asarray(2.0 ** (-8.0 * np.arange(1, n_heads + 1) / n_heads), dtype=jnp.float32)

def diff_attention(q, k, v, lam, subln_gain, lambda_init):
    b_, s_ = q.shape[:2]
    n_qblocks = s_ // Q_BLOCK
    scale = ATTN_HEAD_DIM ** -0.5
    qb = (q * scale).reshape(b_, n_qblocks, Q_BLOCK, N_ATTN_HEADS, 2, ATTN_HEAD_DIM)
    qb = qb.transpose(1, 0, 3, 4, 2, 5)
    kt = k.transpose(0, 2, 3, 1, 4)
    vt = v.transpose(0, 2, 1, 3)
    slopes = alibi_slopes(N_ATTN_HEADS)
    kpos = jnp.arange(s_)

    def block(args):
        q_blk, i = args
        qpos = i * Q_BLOCK + jnp.arange(Q_BLOCK)
        dist = (qpos[:, None] - kpos[None, :]).astype(jnp.float32)
        bias = jnp.where(dist >= 0, -slopes[:, None, None] * dist, -jnp.inf)
        scores = jnp.einsum('bhmqd,bhmkd->bhmqk', q_blk, kt).astype(jnp.float32)
        scores = scores + bias[None, :, None]
        p = jax.nn.softmax(scores, axis=-1)
        a = p[:, :, 0] - lam * p[:, :, 1]
        return jnp.einsum('bhqk,bhkv->bhqv', a.astype(vt.dtype), vt)

    o = lax.map(block, (qb, jnp.arange(n_qblocks)))
    o = o.transpose(1, 0, 3, 2, 4).reshape(b_, s_, N_ATTN_HEADS, ATTN_VALUE_DIM)
    o = rmsnorm(o, subln_gain) * (1.0 - lambda_init)
    return o.reshape(b_, s_, ATTN_WIDTH)

def s5_branch(u, lam_re, lam_im, log_dt, b_re, b_im, c_re, c_im, d_skip, w_glu, b_glu, ssm_gain):
    b_, s_ = u.shape[:2]
    f32 = jnp.float32
    uf = u.astype(f32).reshape(b_, s_, N_SSM_GROUPS, SSM_GROUP)
    lam = lax.complex(lam_re.astype(f32), lam_im.astype(f32))
    dt = jnp.exp(log_dt.astype(f32))[:, None]
    lam_bar = jnp.exp(lam * dt)
    b_c = lax.complex(b_re.astype(f32), b_im.astype(f32))
    b_bar = ((lam_bar - 1.0) / lam)[..., None] * b_c
    bu = jnp.einsum('gnc,bsgc->bsgn', b_bar, uf.astype(jnp.complex64))
    a = jnp.broadcast_to(lam_bar, bu.shape)

    def combine(left, right):
        a_l, b_l = left
        a_r, b_r = right
        return a_r * a_l, a_r * b_l + b_r

    _, states = lax.associative_scan(combine, (a, bu), axis=1)
    c_c = lax.complex(c_re.astype(f32), c_im.astype(f32))
    y = jnp.einsum('gcn,bsgn->bsgc', c_c, states).real + d_skip.astype(f32) * uf
    y = jax.nn.gelu(y.reshape(b_, s_, SSM_WIDTH))
    y = y * jax.nn.sigmoid(y @ w_glu.astype(f32) + b_glu.astype(f32))
    return rmsnorm(y, ssm_gain).astype(u.dtype)

def hier_moe(h, w_router_group, b_router_group, w_router_expert, b_router_expert, w_gate, w_up, w_down):
    n_tok = h.shape[0]
    hf = h.astype(jnp.float32)
    g_logits = hf @ w_router_group.astype(jnp.float32) + b_router_group.astype(jnp.float32)
    g_prob = jax.nn.softmax(g_logits, axis=-1)
    g_sel = jnp.argmax(g_logits, axis=-1)
    p_group = jnp.take_along_axis(g_prob, g_sel[:, None], axis=1)
    e_logits = (hf @ w_router_expert.astype(jnp.float32) + b_router_expert.astype(jnp.float32))
    e_logits = e_logits.reshape(n_tok, N_EXPERT_GROUPS, EXPERTS_PER_GROUP)
    e_in = jnp.take_along_axis(e_logits, g_sel[:, None, None], axis=1)[:, 0]
    e_prob = jax.nn.softmax(e_in, axis=-1)
    top_p, top_i = lax.top_k(e_prob, TOP_K_INNER)
    gates = p_group * top_p
    expert_id = g_sel[:, None] * EXPERTS_PER_GROUP + top_i

    n_assign = n_tok * TOP_K_INNER
    flat_e = expert_id.reshape(-1)
    flat_tok = jnp.repeat(jnp.arange(n_tok), TOP_K_INNER)
    flat_g = gates.reshape(-1)
    order = jnp.argsort(flat_e)
    se, stok, sg = flat_e[order], flat_tok[order], flat_g[order]
    counts = jnp.bincount(flat_e, length=N_EXPERTS)
    start = jnp.cumsum(counts) - counts
    padded = ((counts + MOE_BLOCK - 1) // MOE_BLOCK) * MOE_BLOCK
    pend = jnp.cumsum(padded)
    pstart = pend - padded
    dest = pstart[se] + (jnp.arange(n_assign) - start[se])
    n_rows = ((n_assign + N_EXPERTS * (MOE_BLOCK - 1) + MOE_BLOCK - 1) // MOE_BLOCK) * MOE_BLOCK
    n_blocks = n_rows // MOE_BLOCK
    rows = jnp.zeros((n_rows, h.shape[1]), h.dtype).at[dest].set(h[stok])
    block_e = jnp.minimum(jnp.searchsorted(pend, jnp.arange(n_blocks) * MOE_BLOCK, side='right'), N_EXPERTS - 1)

    def expert_block(args):
        xb, e = args
        hid = jax.nn.silu(xb @ w_gate[e]) * (xb @ w_up[e])
        return hid @ w_down[e]

    out = lax.map(expert_block, (rows.reshape(n_blocks, MOE_BLOCK, -1), block_e)).reshape(n_rows, -1)
    return jax.ops.segment_sum(out[dest] * sg[:, None].astype(out.dtype), stok, num_segments=n_tok)

def setup_inputs(seed: int = 0) -> dict:
    key = jax.random.key(seed)
    ks = jax.random.split(key, 32)
    f32 = jnp.float32
    L, D = DEPTH, D_MODEL
    nrm = lambda k, shape, s: jax.random.normal(k, shape, f32) * s
    n_idx = jnp.arange(SSM_STATE, dtype=f32)
    return {
        "x": jax.random.normal(ks[0], (BATCH, SEQ, D), f32),
        "norm_attn": 1.0 + nrm(ks[1], (L, D), 0.02),
        "w_in": nrm(ks[2], (L, D, IN_COLS), D ** -0.5),
        "lambda_q1": nrm(ks[3], (L, ATTN_HEAD_DIM), 0.1),
        "lambda_k1": nrm(ks[4], (L, ATTN_HEAD_DIM), 0.1),
        "lambda_q2": nrm(ks[5], (L, ATTN_HEAD_DIM), 0.1),
        "lambda_k2": nrm(ks[6], (L, ATTN_HEAD_DIM), 0.1),
        "attn_subln": 1.0 + nrm(ks[7], (L, ATTN_VALUE_DIM), 0.02),
        "ssm_lam_re": -0.5 + nrm(ks[8], (L, N_SSM_GROUPS, SSM_STATE), 0.01),
        "ssm_lam_im": math.pi * n_idx + nrm(ks[9], (L, N_SSM_GROUPS, SSM_STATE), 0.01),
        "ssm_log_dt": jax.random.uniform(ks[10], (L, N_SSM_GROUPS), f32, math.log(DT_MIN), math.log(DT_MAX)),
        "ssm_b_re": nrm(ks[11], (L, N_SSM_GROUPS, SSM_STATE, SSM_GROUP), (2 * SSM_GROUP) ** -0.5),
        "ssm_b_im": nrm(ks[12], (L, N_SSM_GROUPS, SSM_STATE, SSM_GROUP), (2 * SSM_GROUP) ** -0.5),
        "ssm_c_re": nrm(ks[13], (L, N_SSM_GROUPS, SSM_GROUP, SSM_STATE), (2 * SSM_STATE) ** -0.5),
        "ssm_c_im": nrm(ks[14], (L, N_SSM_GROUPS, SSM_GROUP, SSM_STATE), (2 * SSM_STATE) ** -0.5),
        "ssm_d": nrm(ks[15], (L, N_SSM_GROUPS, SSM_GROUP), 1.0),
        "w_glu": nrm(ks[16], (L, SSM_WIDTH, SSM_WIDTH), SSM_WIDTH ** -0.5),
        "b_glu": nrm(ks[17], (L, SSM_WIDTH), 0.01),
        "ssm_norm": 1.0 + nrm(ks[18], (L, SSM_WIDTH), 0.02),
        "w_out": nrm(ks[19], (L, MIX_WIDTH, D), MIX_WIDTH ** -0.5),
        "norm_moe": 1.0 + nrm(ks[20], (L, D), 0.02),
        "w_router_group": nrm(ks[21], (L, D, N_EXPERT_GROUPS), D ** -0.5),
        "b_router_group": nrm(ks[22], (L, N_EXPERT_GROUPS), 0.01),
        "w_router_expert": nrm(ks[23], (L, D, N_EXPERTS), D ** -0.5),
        "b_router_expert": nrm(ks[24], (L, N_EXPERTS), 0.01),
        "w_gate": nrm(ks[25], (L, N_EXPERTS, D, EXPERT_FF), D ** -0.5),
        "w_up": nrm(ks[26], (L, N_EXPERTS, D, EXPERT_FF), D ** -0.5),
        "w_down": nrm(ks[27], (L, N_EXPERTS, EXPERT_FF, D), EXPERT_FF ** -0.5),
        "norm_final": 1.0 + nrm(ks[28], (D,), 0.02),
    }

def reference(x, norm_attn, w_in, lambda_q1, lambda_k1, lambda_q2, lambda_k2, attn_subln,
              ssm_lam_re, ssm_lam_im, ssm_log_dt, ssm_b_re, ssm_b_im, ssm_c_re, ssm_c_im, ssm_d,
              w_glu, b_glu, ssm_norm, w_out, norm_moe, w_router_group, b_router_group,
              w_router_expert, b_router_expert, w_gate, w_up, w_down, norm_final):
    b_, s_, d_ = x.shape
    for l in range(DEPTH):
        h = rmsnorm(x, norm_attn[l])
        proj = h @ w_in[l]
        q = proj[..., :ATTN_WIDTH].reshape(b_, s_, N_ATTN_HEADS, 2, ATTN_HEAD_DIM)
        k = proj[..., ATTN_WIDTH:2 * ATTN_WIDTH].reshape(b_, s_, N_ATTN_HEADS, 2, ATTN_HEAD_DIM)
        v = proj[..., 2 * ATTN_WIDTH:3 * ATTN_WIDTH].reshape(b_, s_, N_ATTN_HEADS, ATTN_VALUE_DIM)
        u = proj[..., 3 * ATTN_WIDTH:]
        lam_init = lambda_init_fn(l)
        lam = (jnp.exp(jnp.sum(lambda_q1[l].astype(jnp.float32) * lambda_k1[l].astype(jnp.float32)))
               - jnp.exp(jnp.sum(lambda_q2[l].astype(jnp.float32) * lambda_k2[l].astype(jnp.float32)))
               + lam_init)
        attn_out = diff_attention(q, k, v, lam, attn_subln[l], lam_init)
        ssm_out = s5_branch(u, ssm_lam_re[l], ssm_lam_im[l], ssm_log_dt[l], ssm_b_re[l], ssm_b_im[l],
                            ssm_c_re[l], ssm_c_im[l], ssm_d[l], w_glu[l], b_glu[l], ssm_norm[l])
        x = x + jnp.concatenate([attn_out, ssm_out], axis=-1) @ w_out[l]
        h = rmsnorm(x, norm_moe[l]).reshape(b_ * s_, d_)
        x = x + hier_moe(h, w_router_group[l], b_router_group[l], w_router_expert[l], b_router_expert[l],
                         w_gate[l], w_up[l], w_down[l]).reshape(b_, s_, d_)
    return rmsnorm(x, norm_final)


_drawn_inputs = setup_inputs


def setup_inputs(seed=0):
    import zlib

    import numpy as np

    out = dict(_drawn_inputs(seed))
    spreads = {}
    factors = {'lambda_q1': 3.684,
     'lambda_k1': 2.846,
     'lambda_q2': 8.0,
     'attn_subln': 4.919,
     'ssm_lam_re': 8.0,
     'b_glu': 8.0,
     'ssm_norm': 4.341,
     'norm_moe': 4.752,
     'b_router_group': 5.578,
     'b_router_expert': 8.0,
     'norm_final': 2.738}
    for name, (base, spread) in spreads.items():
        noise = np.random.default_rng([zlib.crc32(name.encode()), seed]).standard_normal(out[name].shape)
        drawn = base * np.exp(spread * noise) if base else spread * noise
        out[name] = __import__('jax').numpy.asarray(drawn.astype(out[name].dtype))
    for name, factor in factors.items():
        out[name] = (out[name] * factor).astype(out[name].dtype)
    return out
```

```python
from contextlib import ExitStack, contextmanager
import math

import numpy as np
import concourse.bass as bass
import concourse.mybir as mybir

F32 = mybir.dt.float32
I32 = mybir.dt.int32
ALU = mybir.AluOpType
ACT = mybir.ActivationFunctionType
AX = mybir.AxisListType

P = 128
SEQ = 2048
D = 1024
KT = D // P
NT = SEQ // P
HEADS = 4
HD = 64
VD = 128
SW = 512
NG = 32
GC = 16
NS = 64
CH = 8
NCH = SEQ // CH
GB = 8
NB = NG // GB
BANK = 512
EPS = 1e-6
LAM_INIT = 0.8 - 0.6 * math.exp(-0.3 * 0)
NE = 32
NEG = 4
EPG = 8
FF = 512
NBLK = 64
MIN_BLK = 2 * SEQ // P
BIG = 3.0e38


@contextmanager
def phase_semaphores(nc):
    taken = []

    def sem(name):
        taken.append(nc.alloc_semaphore(name=name))
        return taken[-1]

    yield sem
    nc.clear_and_free_semaphores(taken)
    nc.all_engine_barrier()


class Step:

    def __init__(self, eng, sem, start=0):
        self.eng, self.sem, self.n = eng, sem, start

    def __call__(self, ins):
        self.n += 1
        ins.then_inc(self.sem, 1)
        self.eng.wait_ge(self.sem, self.n)


def exact_exp(step, eng, out, x, n, q, ni):
    magic = 12582912.0
    step(eng.tensor_scalar(n, x, 1.4426950408889634, -126.0, ALU.mult, ALU.max))
    step(eng.tensor_scalar(n, n, 127.0, magic, ALU.min, ALU.add))
    step(eng.tensor_scalar(n, n, -magic, None, ALU.add))
    step(eng.scalar_tensor_tensor(x, n, -0.693359375, x, ALU.mult, ALU.add))
    step(eng.scalar_tensor_tensor(x, n, 2.12194440e-4, x, ALU.mult, ALU.add))
    step(eng.tensor_scalar(q, x, 1.0 / 40320, None, ALU.mult))
    for k in range(7, 0, -1):
        step(eng.scalar_tensor_tensor(q, q, 1.0 / math.factorial(k), x, ALU.add, ALU.mult))
    step(eng.tensor_scalar(n, n, 127.0, None, ALU.add))
    step(eng.tensor_copy(ni, n))
    step(eng.tensor_scalar(ni, ni, 23, None, ALU.logical_shift_left))
    step(eng.scalar_tensor_tensor(out, q, 1.0, ni.bitcast(F32), ALU.add, ALU.mult))


def complex_mul(step, eng, orr, oi, ar, ai, br, bi, t):
    step(eng.tensor_tensor(orr, ar, br, ALU.mult))
    step(eng.tensor_tensor(t, ai, bi, ALU.mult))
    step(eng.tensor_tensor(orr, orr, t, ALU.subtract))
    step(eng.tensor_tensor(oi, ar, bi, ALU.mult))
    step(eng.tensor_tensor(t, ai, br, ALU.mult))
    step(eng.tensor_tensor(oi, oi, t, ALU.add))


def norm_project_prepare(nc, ident, r8, a, d):
    chunks = [3, 0, 1, 2]
    with ExitStack() as ctx:
        sb = lambda name, shape, dt=F32: ctx.enter_context(nc.sbuf_tensor(name, shape, dt))
        sem = ctx.enter_context(phase_semaphores(nc))
        bank = [ctx.enter_context(nc.psum_tensor(f"a_bank{i}", [P, BANK], F32)) for i in range(8)]
        hT = sb("hT", [P, KT, SEQ])
        w = sb("w_in_chunk", [P, 2, KT, SW])
        x = sb("x_tile", [P, 3, D])
        xn = sb("xn_tile", [P, 2, D])
        gain = sb("gain_attn", [P, D])
        ss = sb("sumsq_a", [P, NT])
        rstd = sb("rstd_a", [P, NT])
        ev = sb("proj_out", [P, 4, BANK])
        lamin = sb("lamin", [NG, 2, 2, NS])
        cin = sb("cin", [P, 2, NB, 2, NS])
        B1, B2, B1b, B2b = (sb(f"b{n}", [P, NG, GC]) for n in ("1", "2", "1bar", "2bar"))
        tb = sb("tb", [P, NG, GC])
        C1, C2 = sb("C1", [P, NG, GC]), sb("C2", [P, NG, GC])
        Dm = sb("Dm", [P, NG, GC])
        sm = sb("small", [P, 24, NG])
        smi = sb("small_int", [P, NG], I32)
        PR, PI = sb("pow_re", [P, NG, CH + 1]), sb("pow_im", [P, NG, CH + 1])
        PRr, PIr = sb("pow_re_rev", [P, NG, CH]), sb("pow_im_rev", [P, NG, CH])
        tp = sb("tp", [P, NG, CH // 2])
        anc = sb("anchor", [P, 8, 2, NG])
        TC, TS, TT = (sb(f"table_{n}", [P, GB, NCH]) for n in ("cos", "sin", "tmp"))
        Wn, Qn, Q2n = (sb(f"mat_{n}", [P, GB, CH, GC]) for n in ("w", "q", "q2"))
        junk = TT[:, 0:4, :].rearrange("p g m -> p (g m)")
        Wt = TT[:, 4:8, :].rearrange("p a (b k c) -> p (a b) k c", b=2, c=GC)
        W1, W2 = sb("mat_w1", [P, GB, P]), sb("mat_w2", [P, GB, P])
        Kt = sb("kernel_taps", [P, NG, GC])
        x_in = [sem(f"x_in{i}") for i in range(3)]
        w_in_s = [sem(f"w_in{i}") for i in range(2)]
        gain_in, param_in, bc_in = sem("gain_in"), sem("param_in"), sem("bc_in")
        sq_done, rstd_step, sqrt_done, xn_done = sem("sq_done"), sem("rstd_step"), sem("sqrt_done"), sem("xn_done")
        hT_psum, hT_done = sem("hT_psum"), sem("hT_done")
        proj_done, ev_done = sem("proj_done"), sem("ev_done")
        stored = [sem(f"proj_stored{i}") for i in range(4)]
        par_T, par_T_used, prep = sem("par_T"), sem("par_T_used"), sem("prep_step")
        sin_in, sin_out, mats, wT, wT_used = (sem(n) for n in ("sin_in", "sin_out", "mats_ready", "wT", "wT_used"))
        mats_w, d_masked = sem("mats_w"), sem("d_masked")
        mats_stored, w12_stored, taps, taps_done, taps_stored, small_in = (
            sem(n) for n in ("mats_stored", "w12_stored", "taps", "taps_done", "taps_stored", "small_in"))
        UNITS = 64
        PB = 3
        BATCH_AT = [24 + 8 * b for b in range(NB)]
        with nc.Block() as block:

            @block.sync
            def _(sp):
                for half in range(2):
                    sp.dma_start(lamin[:, 0, half, :], a["ssm_lam_re"][0]).then_inc(param_in, 16)
                    sp.dma_start(lamin[:, 1, half, :], a["ssm_lam_im"][0]).then_inc(param_in, 16)
                for v, halves in enumerate((("ssm_c_re", "ssm_c_im"), ("ssm_c_im", "ssm_c_re"))):
                    for half, name in enumerate(halves):
                        sp.dma_start(cin[:, v, :, half, :],
                                     a[name][0].rearrange("(b g) c n -> (g c) b n", g=GB)).then_inc(param_in, 16)
                sp.dma_start(gain[:], a["norm_attn"].to_broadcast([P, D])).then_inc(gain_in, 16)
                for i in range(NT):
                    if i >= 3:
                        sp.wait_ge(xn_done, i - 2)
                    sp.dma_start(x[:, i % 3, :], a["x"][0, i * P:(i + 1) * P, :]).then_inc(x_in[i % 3], 16)
                for half in range(2):
                    part = slice(half * NS, (half + 1) * NS)
                    sp.dma_start(B1[part], a["ssm_b_im" if half else "ssm_b_re"][0].rearrange("g n c -> n g c")).then_inc(bc_in, 16)
                    sp.dma_start(B2[part], a["ssm_b_re" if half else "ssm_b_im"][0].rearrange("g n c -> n g c")).then_inc(bc_in, 16)
                for n in range(UNITS):
                    c, k = chunks[n // 16], n % 16
                    sp.wait_ge(ev_done, n + 1)
                    if c == 3:
                        dst = d["u"][k // 8, k % 8]
                    elif c == 2:
                        dst = d["v"][k * P:(k + 1) * P, :]
                    else:
                        dst = d["qT" if c == 0 else "kT"][k // 4, :, (k % 4) * BANK:(k % 4 + 1) * BANK]
                    sp.dma_start(dst, ev[:, n % 4, :]).then_inc(stored[n % 4], 16)
                for s in range(4):
                    sp.wait_ge(stored[s], 16 * UNITS // 4)
                sp.wait_ge(taps_done, 1)
                for i in range(CH):
                    sp.dma_start(d["taps"][CH - 1 - i], Kt[i * GC:(i + 1) * GC]).then_inc(taps_stored, 16)
                sp.wait_ge(taps_stored, 16 * CH)

            @block.gpsimd
            def _(pool):
                pool.dma_start(sm[:, 0, :], a["ssm_log_dt"].to_broadcast([P, NG])).then_inc(small_in, 16)
                pool.dma_start(Dm[:], a["ssm_d"].rearrange("l g c -> l (g c)").to_broadcast([P, NG * GC]).rearrange("p (g c) -> p g c", g=NG)).then_inc(small_in, 16)
                pool.wait_ge(small_in, 32)
                pool.affine_select(out=Dm[:], in_=Dm[:], pattern=[[0, NG], [-1, GC]], compare_op=ALU.is_equal,
                                   fill=0.0, base=-(P - GC), channel_multiplier=1).then_inc(d_masked, 1)
                for n, c in enumerate(chunks):
                    if n >= 2:
                        pool.wait_ge(proj_done, 16 * (n - 1))
                    pool.dma_start(w[:, n % 2], a["w_in"][0].rearrange("(p k) n -> p k n", k=KT)[:, :, c * SW:(c + 1) * SW]
                                   ).then_inc(w_in_s[n % 2], 16)

            @block.scalar
            def _(act):
                act.wait_ge(par_T, 1)
                step = Step(act, par_T_used)
                step(act.activation(sm[:, 1:3, :], bank[0][:, 0:2 * NG].rearrange("p (a g) -> p a g", a=2), ACT.Copy))
                c1v, c2v = (bank[i][:].rearrange("p (g c) -> p g c", g=NG) for i in (1, 2))
                step(act.activation(C1[0:NS], c1v[0:NS], ACT.Copy))
                step(act.activation(C1[NS:P], c1v[NS:P], ACT.Copy, scale=-1.0))
                step(act.activation(C2[:], c2v, ACT.Copy, scale=-1.0))
                for i in range(NT):
                    act.wait_ge(x_in[i % 3], 16 * (i // 3 + 1))
                    if i:
                        act.wait_ge(sq_done, i)
                    act.activation(junk, x[:, i % 3, :], ACT.Square, accum_out=ss[:, i:i + 1]).then_inc(sq_done, 1)
                    act.wait_ge(rstd_step, 2 * i + 1)
                    act.activation(rstd[:, i:i + 1], rstd[:, i:i + 1], ACT.Sqrt).then_inc(sqrt_done, 1)
                    for h in range(2):
                        n = 2 * i - 2 + h
                        if n >= 0:
                            act.wait_ge(hT_psum, n + 1)
                            act.activation(hT[:, 4 * h:4 * h + 4, (i - 1) * P:i * P],
                                           bank[n % 4][:].rearrange("p (k t) -> p k t", k=4), ACT.Copy).then_inc(hT_done, 1)
                for h in range(2):
                    n = 2 * NT - 2 + h
                    act.wait_ge(hT_psum, n + 1)
                    act.activation(hT[:, 4 * h:4 * h + 4, (NT - 1) * P:NT * P],
                                   bank[n % 4][:].rearrange("p (k t) -> p k t", k=4), ACT.Copy).then_inc(hT_done, 1)

                def sines():
                    act.wait_ge(sin_in, 1)
                    act.activation(sm[:, 7:9, :], sm[:, 7:9, :], ACT.Sin).then_inc(sin_out, 1)

                def batch(b):
                    for q in range(2):
                        act.wait_ge(wT, 2 * b + q + 1)
                        if b and q == 0:
                            act.wait_ge(w12_stored, 32 * b)
                        v = bank[2 * (b % 2) + q][:].rearrange("p (g n) -> p g n", g=4)
                        gs = slice(4 * q, 4 * q + 4)
                        act.activation(W1[:, gs, :], v, ACT.Copy).then_inc(wT_used, 1)
                        act.activation(W2[:, gs, 0:NS], v[:, :, NS:P], ACT.Copy).then_inc(wT_used, 1)
                        act.activation(W2[:, gs, NS:P], v[:, :, 0:NS], ACT.Copy, scale=-1.0).then_inc(wT_used, 1)
                    act.wait_ge(wT_used, 6 * (b + 1))
                    act.dma_start(d["w1"][b], W1[:]).then_inc(w12_stored, 16)
                    act.dma_start(d["w2"][b], W2[:]).then_inc(w12_stored, 16)
                    act.wait_ge(mats, 2 * (b + 1))
                    for name, t in (("q", Qn), ("q2", Q2n), ("cos", TC), ("sin", TS)):
                        act.dma_start(d[name][b], t[:]).then_inc(mats_stored, 16)

                sines()
                for n in range(UNITS):
                    if n in BATCH_AT:
                        batch(BATCH_AT.index(n))
                    act.wait_ge(proj_done, n + 1)
                    if n >= 4:
                        act.wait_ge(stored[n % 4], 16 * (n // 4))
                    act.activation(ev[:, n % 4, :], bank[4 + n % PB][:], ACT.Copy,
                                   scale=HD ** -0.5 if chunks[n // 16] == 0 else 1.0).then_inc(ev_done, 1)
                act.wait_ge(w12_stored, 32 * NB)
                act.wait_ge(mats_stored, 64 * NB)

            @block.vector
            def _(dve):
                for i in range(NT):
                    dve.wait_ge(sq_done, i + 1)
                    dve.tensor_scalar(rstd[:, i:i + 1], ss[:, i:i + 1], 1.0 / D, EPS, ALU.mult, ALU.add).then_inc(rstd_step, 1)
                    dve.wait_ge(sqrt_done, i + 1)
                    dve.reciprocal(rstd[:, i:i + 1], rstd[:, i:i + 1]).then_inc(rstd_step, 1)
                    dve.wait_ge(rstd_step, 2 * i + 2)
                    if i == 0:
                        dve.wait_ge(gain_in, 16)
                    if i >= 2:
                        dve.wait_ge(hT_psum, 2 * (i - 1))
                    dve.scalar_tensor_tensor(xn[:, i % 2, :], x[:, i % 3, :], rstd[:, i:i + 1], gain[:],
                                             ALU.mult, ALU.mult).then_inc(xn_done, 1)
                step = Step(dve, prep)
                s = lambda k: sm[:, k, :]
                dve.wait_ge(small_in, 32)
                dve.wait_ge(par_T_used, 4)
                dve.wait_ge(d_masked, 1)
                exact_exp(step, dve, s(3), s(0), s(4), s(5), smi[:])
                step(dve.tensor_tensor(s(4), s(1), s(3), ALU.mult))
                step(dve.tensor_tensor(s(7), s(2), s(3), ALU.mult))
                exact_exp(step, dve, s(5), s(4), s(6), s(9), smi[:])
                step(dve.tensor_scalar(s(6), s(7), 1.0 / (2 * math.pi), 12582912.0, ALU.mult, ALU.add))
                step(dve.tensor_scalar(s(6), s(6), -12582912.0, None, ALU.add))
                two_pi = [6.28125, 0.0019350051879882812, 3.01991623e-07]
                for c in two_pi:
                    step(dve.scalar_tensor_tensor(s(7), s(6), -c, s(7), ALU.mult, ALU.add))
                step(dve.tensor_scalar(s(7), s(7), 3.1415925, -3.1415925, ALU.min, ALU.max))
                step(dve.tensor_scalar(s(8), s(7), -1.0, None, ALU.mult))
                step(dve.tensor_tensor(s(8), s(7), s(8), ALU.max))
                dve.tensor_scalar(s(8), s(8), -1.0, math.pi / 2, ALU.mult, ALU.add).then_inc(sin_in, 1)
                dve.wait_ge(sin_out, 1)
                step(dve.tensor_tensor(PR[:, :, 1], s(5), s(8), ALU.mult))
                step(dve.tensor_tensor(PI[:, :, 1], s(5), s(7), ALU.mult))
                step(dve.memset(PR[:, :, 0], 1.0))
                step(dve.memset(PI[:, :, 0], 0.0))
                step(dve.tensor_tensor(s(10), s(1), s(1), ALU.mult))
                step(dve.tensor_tensor(s(11), s(2), s(2), ALU.mult))
                step(dve.tensor_tensor(s(10), s(10), s(11), ALU.add))
                step(dve.reciprocal(s(10), s(10)))
                step(dve.tensor_scalar(s(11), PR[:, :, 1], -1.0, None, ALU.add))
                step(dve.tensor_tensor(s(12), s(11), s(1), ALU.mult))
                step(dve.tensor_tensor(s(13), PI[:, :, 1], s(2), ALU.mult))
                step(dve.tensor_tensor(s(12), s(12), s(13), ALU.add))
                step(dve.tensor_tensor(s(12), s(12), s(10), ALU.mult))
                step(dve.tensor_tensor(s(13), PI[:, :, 1], s(1), ALU.mult))
                step(dve.tensor_tensor(s(14), s(11), s(2), ALU.mult))
                step(dve.tensor_tensor(s(13), s(13), s(14), ALU.subtract))
                step(dve.tensor_tensor(s(13), s(13), s(10), ALU.mult))
                dve.wait_ge(bc_in, 64)
                step(dve.tensor_scalar(B2[0:NS], B2[0:NS], -1.0, None, ALU.mult))
                fr = s(12).rearrange("p (g o) -> p g o", o=1).to_broadcast([P, NG, GC])
                fi = s(13).rearrange("p (g o) -> p g o", o=1).to_broadcast([P, NG, GC])
                step(dve.tensor_tensor(B1b[:], B1[:], fr, ALU.mult))
                step(dve.tensor_tensor(tb[:], B2[:], fi, ALU.mult))
                step(dve.tensor_tensor(B1b[:], B1b[:], tb[:], ALU.add))
                step(dve.tensor_tensor(B2b[:], B2[:], fr, ALU.mult))
                step(dve.tensor_tensor(tb[:], B1[:], fi, ALU.mult))
                step(dve.tensor_tensor(B2b[:], B2b[:], tb[:], ALU.subtract))
                k = 1
                while k < CH:
                    br, bi = (t[:, :, k:k + 1].to_broadcast([P, NG, k]) for t in (PR, PI))
                    complex_mul(step, dve, PR[:, :, k + 1:2 * k + 1], PI[:, :, k + 1:2 * k + 1],
                                PR[:, :, 1:k + 1], PI[:, :, 1:k + 1], br, bi, tp[:, :, 0:k])
                    k *= 2
                for i in range(CH):
                    step(dve.tensor_copy(PRr[:, :, i], PR[:, :, CH - 1 - i]))
                    step(dve.tensor_copy(PIr[:, :, i], PI[:, :, CH - 1 - i]))
                step(dve.tensor_tensor(s(15), s(5), s(5), ALU.mult))
                step(dve.tensor_tensor(s(15), s(15), s(15), ALU.mult))
                step(dve.tensor_tensor(r8[:], s(15), s(15), ALU.mult))
                cur = (s(8), s(7))
                for k in range(11):
                    if k < 3:
                        nxt = (s(16 + 2 * (k % 2)), s(17 + 2 * (k % 2)))
                        if k == 2:
                            nxt = (anc[:, 0, 0, :], anc[:, 0, 1, :])
                    elif k < 10:
                        nxt = (anc[:, k - 2, 0, :], anc[:, k - 2, 1, :])
                    else:
                        break
                    complex_mul(step, dve, nxt[0], nxt[1], cur[0], cur[1], cur[0], cur[1], s(20))
                    step(dve.tensor_tensor(s(20), nxt[0], nxt[0], ALU.mult))
                    step(dve.tensor_tensor(s(21), nxt[1], nxt[1], ALU.mult))
                    step(dve.tensor_tensor(s(20), s(20), s(21), ALU.add))
                    step(dve.tensor_scalar(s(20), s(20), -0.5, 1.5, ALU.mult, ALU.add))
                    step(dve.tensor_tensor(nxt[0], nxt[0], s(20), ALU.mult))
                    step(dve.tensor_tensor(nxt[1], nxt[1], s(20), ALU.mult))
                    cur = nxt
                for b in range(NB):
                    gs = slice(b * GB, (b + 1) * GB)
                    up = lambda t: t.rearrange("p g (k o) -> p g k o", o=1).to_broadcast([P, GB, CH, GC])
                    across = lambda t: t.rearrange("p g (o c) -> p g o c", o=1).to_broadcast([P, GB, CH, GC])
                    if b:
                        dve.wait_ge(mats_stored, 64 * b)
                        dve.wait_ge(taps, b)
                    step(dve.tensor_tensor(Wn[:], up(PRr[:, gs]), across(B1b[:, gs]), ALU.mult))
                    step(dve.tensor_tensor(Wt, up(PIr[:, gs]), across(B2b[:, gs]), ALU.mult))
                    dve.tensor_tensor(Wn[:], Wn[:], Wt, ALU.add).then_inc(mats_w, 1)
                    dve.wait_ge(mats_w, b + 1)
                    step(dve.tensor_tensor(Qn[:], up(PR[:, gs, 1:]), across(C1[:, gs]), ALU.mult))
                    step(dve.tensor_tensor(Wt, up(PI[:, gs, 1:]), across(C2[:, gs]), ALU.mult))
                    step(dve.tensor_tensor(Qn[:], Qn[:], Wt, ALU.add))
                    step(dve.tensor_tensor(Q2n[:], up(PR[:, gs, 1:]), across(C2[:, gs]), ALU.mult))
                    step(dve.tensor_tensor(Wt, up(PI[:, gs, 1:]), across(C1[:, gs]), ALU.mult))
                    dve.tensor_tensor(Q2n[:], Q2n[:], Wt, ALU.subtract).then_inc(mats, 1)
                    step(dve.memset(TC[:, :, 0:1], 1.0))
                    step(dve.memset(TS[:, :, 0:1], 0.0))
                    k = 1
                    for e in range(8):
                        br, bi = (anc[:, e, r, gs].rearrange("p (g o) -> p g o", o=1).to_broadcast([P, GB, k]) for r in (0, 1))
                        complex_mul(step, dve, TC[:, :, k:2 * k], TS[:, :, k:2 * k], TC[:, :, 0:k], TS[:, :, 0:k],
                                    br, bi, TT[:, :, 0:k])
                        k *= 2
                    dve.tensor_copy(TT[:, :, 0:1], TC[:, :, 0:1]).then_inc(mats, 1)
                dve.wait_ge(taps, NB)
                dve.tensor_tensor(Kt[:], bank[7][:].rearrange("p (g c) -> p g c", g=NG), Dm[:],
                                  ALU.add).then_inc(taps_done, 1)

            @block.tensor
            def _(pe):
                pe.wait_ge(param_in, 16 * 8)
                for r in range(2):
                    pe.transpose(bank[0][:, r * NG:(r + 1) * NG], lamin[:, r].rearrange("g h n -> g (h n)"),
                                 ident[0:NG, 0:NG])
                for v in range(2):
                    for b in range(NB):
                        last = pe.transpose(bank[1 + v][:, b * P:(b + 1) * P], cin[:, v, b].rearrange("p h n -> p (h n)"), ident[:])
                last.then_inc(par_T, 1)
                pe.wait_ge(par_T_used, 4)
                for i in range(NT):
                    pe.wait_ge(xn_done, i + 1)
                    for h in range(2):
                        n = 2 * i + h
                        if n >= 4:
                            pe.wait_ge(hT_done, n - 3)
                        for k in range(4):
                            last = pe.transpose(bank[n % 4][:, k * P:(k + 1) * P], xn[:, i % 2, 4 * h + k:D:KT], ident[:])
                        last.then_inc(hT_psum, 1)
                pe.wait_ge(hT_done, 2 * NT)

                def batch(b):
                    pe.wait_ge(mats_w, b + 1)
                    for q in range(2):
                        if b >= 2:
                            pe.wait_ge(wT_used, 6 * (b - 1))
                        for g in range(4):
                            last = pe.transpose(bank[2 * (b % 2) + q][:, g * P:(g + 1) * P],
                                                Wn[:, 4 * q + g].rearrange("p i c -> p (i c)"), ident[:])
                        last.then_inc(wT, 1)

                def tap(b):
                    for g in range(GB):
                        last = pe.matmul(bank[7][:, (b * GB + g) * GC:(b * GB + g + 1) * GC],
                                         Wn[:, g].rearrange("p i c -> p (i c)"), C1[:, b * GB + g], start=True, stop=True)
                    last.then_inc(taps, 1)

                for n in range(UNITS):
                    c, k = chunks[n // 16], n % 16
                    if n in BATCH_AT:
                        batch(BATCH_AT.index(n))
                        tap(BATCH_AT.index(n))
                    if k == 0:
                        pe.wait_ge(w_in_s[(n // 16) % 2], 16 * (n // 32 + 1))
                    if n >= PB:
                        pe.wait_ge(ev_done, n - PB + 1)
                    wc = w[:, (n // 16) % 2]
                    for kt in range(KT):
                        if c == 3:
                            lhsT, rhs = hT[:, kt, (k // 8) * 1024 + k % 8:(k // 8 + 1) * 1024:CH], wc[:, kt, :]
                        elif c == 2:
                            lhsT, rhs = hT[:, kt, k * P:(k + 1) * P], wc[:, kt, :]
                        else:
                            lhsT, rhs = wc[:, kt, (k // 4) * P:(k // 4 + 1) * P], hT[:, kt, (k % 4) * BANK:(k % 4 + 1) * BANK]
                        last = pe.matmul(bank[4 + n % PB][:], lhsT, rhs, start=kt == 0, stop=kt == KT - 1)
                    last.then_inc(proj_done, 1)


def s5_groups(nc, ident, r8, U, a, d):
    NP = NG // 2
    with ExitStack() as ctx:
        sb = lambda name, shape, dt=F32: ctx.enter_context(nc.sbuf_tensor(name, shape, dt))
        sem = ctx.enter_context(phase_semaphores(nc))
        bank = [ctx.enter_context(nc.psum_tensor(f"b_bank{i}", [P, BANK], F32)) for i in range(8)]
        Ut = sb("u_by_group", [P, 2, NG, CH, GC])
        M = sb("taps_toeplitz", [P, CH, SW])
        Wb = sb("w_batch", [P, 2, 2, GB, P])
        Qb = sb("q_batch", [P, 2, 2, GB, CH * GC])
        Tb = sb("table_batch", [P, 2, 2, GB, NCH])
        Ug = sb("u_group", [P, 2, 2, NCH])
        zi = sb("z_in", [P, 2, 2, NCH])
        zt = sb("z_tmp", [P, 2, NCH])
        z = sb("z_state", [P, 2, 2, NCH])
        cz, sz = sb("cos_z", [P, 2, 2, NCH]), sb("sin_z", [P, 2, 2, NCH])
        u_in = [sem(f"u_in{i}") for i in range(2)]
        m_zero, m_in, regrouped = sem("m_zero"), sem("m_in"), sem("regrouped")
        batch_in = [sem(f"batch_in{i}") for i in range(2)]
        uT, ug_ready, v_done = sem("uT"), sem("ug_ready"), sem("v_done")
        v_used, z_in_done, z_done, cz_zero, cz_done, sz_done = (
            sem(n) for n in ("v_used", "z_in_done", "z_done", "cz_zero", "cz_done", "sz_done"))
        y_done, y_used = sem("y_done"), sem("y_used")
        with nc.Block() as block:

            @block.sync
            def _(sp):
                for h in range(2):
                    sp.dma_start(U[:, h], d["u"][h].rearrange("j m c -> m j c")).then_inc(u_in[h], 16)
                for b in range(NB):
                    if b >= 2:
                        sp.wait_ge(y_done, 4 * (b - 1))
                    for r, name in enumerate(("w1", "w2")):
                        sp.dma_start(Wb[:, b % 2, r], d[name][b]).then_inc(batch_in[b % 2], 16)
                    for r, name in enumerate(("cos", "sin")):
                        sp.dma_start(Tb[:, b % 2, r], d[name][b]).then_inc(batch_in[b % 2], 16)
                    for r, name in enumerate(("q", "q2")):
                        sp.dma_start(Qb[:, b % 2, r], d[name][b].rearrange("p g k c -> p g (k c)")).then_inc(batch_in[b % 2], 16)
                    if b == 0:
                        sp.wait_ge(m_zero, 1)
                        for i in range(CH):
                            sp.dma_start(M[i * GC:(i + 1) * GC, i:, :], d["taps"][0:CH - i].rearrange("t q g c -> q t (g c)")
                                         ).then_inc(m_in, 16)

            @block.gpsimd
            def _(pool):
                pool.memset(cz[:, :, :, 0:1], 0.0).then_inc(cz_zero, 1)
                pool.memset(sz[:, :, :, 0:1], 0.0).then_inc(cz_zero, 1)
                for p in range(NP):
                    b, g = p // 4, 2 * (p % 4)
                    pool.wait_ge(z_done, 2 * (p + 1))
                    if p >= 2:
                        pool.wait_ge(y_done, p - 1)
                    pool.tensor_tensor(cz[:, p % 2, :, 1:], z[:, p % 2, :, 0:NCH - 1], Tb[:, b % 2, 0, g:g + 2, 0:NCH - 1],
                                       ALU.mult).then_inc(cz_done, 1)
                    pool.tensor_tensor(sz[:, p % 2, :, 1:], z[:, p % 2, :, 0:NCH - 1], Tb[:, b % 2, 1, g:g + 2, 0:NCH - 1],
                                       ALU.mult).then_inc(sz_done, 1)

            @block.vector
            def _(dve):
                dve.memset(M[:], 0.0).then_inc(m_zero, 1)
                for h in range(2):
                    dve.wait_ge(u_in[h], 16)
                    for j in range(CH):
                        dve.tensor_copy(Ut[:, h, :, j], U[:, h, j].rearrange("m (g c) -> m g c", c=GC)).then_inc(regrouped, 1)
                for p in range(NP):
                    b, g = p // 4, 2 * (p % 4)
                    v1, v2 = (bank[2 + 2 * (p % 2) + r][:].rearrange("p (g m) -> p g m", g=2) for r in range(2))
                    dve.wait_ge(v_done, p + 1)
                    if p >= 2:
                        dve.wait_ge(z_done, 2 * (p - 1))
                    if p:
                        dve.wait_ge(z_in_done, p)
                    dve.tensor_tensor(zi[:, p % 2], v1, Tb[:, b % 2, 0, g:g + 2], ALU.mult).then_inc(v_used, 1)
                    dve.tensor_tensor(zt[:], v2, Tb[:, b % 2, 1, g:g + 2], ALU.mult).then_inc(v_used, 1)
                    dve.wait_ge(v_used, 2 * (p + 1))
                    dve.tensor_tensor(zi[:, p % 2], zi[:, p % 2], zt[:], ALU.add).then_inc(z_in_done, 1)
                    dve.wait_ge(z_in_done, p + 1)
                    if p >= 2:
                        dve.wait_ge(sz_done, p - 1)
                        dve.wait_ge(cz_done, p - 1)
                    for e in range(2):
                        G = 2 * p + e
                        dve.tensor_tensor_scan(z[:, p % 2, e], r8[:, G:G + 1].to_broadcast([P, NCH]), zi[:, p % 2, e], 0.0,
                                               ALU.mult, ALU.add).then_inc(z_done, 1)

            @block.scalar
            def _(act):
                def gelu(p):
                    act.wait_ge(y_done, p + 1)
                    if p == 0:
                        act.wait_ge(regrouped, 2 * CH)
                    for e in range(2):
                        G = 2 * p + e
                        y = bank[6 + p % 2][:, e * NCH:(e + 1) * NCH].rearrange("m (h j c) -> m h j c", h=2, c=GC)
                        act.activation(U[:, :, :, G * GC:(G + 1) * GC], y, ACT.Gelu_apprx_tanh).then_inc(y_used, 1)
                for p in range(NP):
                    act.wait_ge(uT, p + 1)
                    if p >= 2:
                        act.wait_ge(y_done, p - 1)
                    act.activation(Ug[:, p % 2], bank[p % 2][:].rearrange("p (g m) -> p g m", g=2), ACT.Copy).then_inc(ug_ready, 1)
                    if p:
                        gelu(p - 1)
                gelu(NP - 1)

            @block.tensor
            def _(pe):
                def states(p):
                    b, g = p // 4, 2 * (p % 4)
                    if p >= 2:
                        pe.wait_ge(ug_ready, p - 1)
                    if p == 0:
                        pe.wait_ge(regrouped, 2 * CH)
                    for e in range(2):
                        for h in range(2):
                            G = 2 * p + e
                            last = pe.transpose(bank[p % 2][:, e * NCH + h * P:e * NCH + (h + 1) * P],
                                                Ut[:, h, G].rearrange("m j c -> m (j c)"), ident[:])
                    last.then_inc(uT, 1)
                    if p % 4 == 0:
                        pe.wait_ge(batch_in[b % 2], 16 * 6 * (b // 2 + 1))
                    pe.wait_ge(ug_ready, p + 1)
                    if p >= 2:
                        pe.wait_ge(v_used, 2 * (p - 1))
                    for r in range(2):
                        for e in range(2):
                            last = pe.matmul(bank[2 + 2 * (p % 2) + r][:, e * NCH:(e + 1) * NCH], Wb[:, b % 2, r, g + e],
                                             Ug[:, p % 2, e], start=True, stop=True)
                    last.then_inc(v_done, 1)

                def outputs(p):
                    b, g = p // 4, 2 * (p % 4)
                    if p == 0:
                        pe.wait_ge(m_in, 16 * CH)
                        pe.wait_ge(cz_zero, 2)
                    if p >= 2:
                        pe.wait_ge(y_used, 2 * (p - 1))
                    pe.wait_ge(cz_done, p + 1)
                    pe.wait_ge(sz_done, p + 1)
                    for e in range(2):
                        G = 2 * p + e
                        for h in range(2):
                            o = bank[6 + p % 2][:, e * NCH + h * P:e * NCH + (h + 1) * P]
                            ms = slice(h * P, (h + 1) * P)
                            pe.matmul(o, Ug[:, p % 2, e, ms], M[:, :, G * GC:(G + 1) * GC], start=True, stop=False)
                            pe.matmul(o, cz[:, p % 2, e, ms], Qb[:, b % 2, 0, g + e], start=False, stop=False)
                            last = pe.matmul(o, sz[:, p % 2, e, ms], Qb[:, b % 2, 1, g + e], start=False, stop=True)
                    last.then_inc(y_done, 1)

                states(0)
                for p in range(NP):
                    if p + 1 < NP:
                        states(p + 1)
                    outputs(p)


def s5_gate(nc, ident, ones, Y, ssmT, srs, a, d):
    with ExitStack() as ctx:
        sb = lambda name, shape, dt=F32: ctx.enter_context(nc.sbuf_tensor(name, shape, dt))
        sem = ctx.enter_context(phase_semaphores(nc))
        bank = [ctx.enter_context(nc.psum_tensor(f"g_bank{i}", [P, BANK], F32)) for i in range(8)]
        yT = sb("yT", [P, 4, SEQ])
        wg = sb("w_glu", [P, 4, SW])
        bg, gg = sb("b_glu", [P, 4]), sb("ssm_gain", [P, 4])
        sg = sb("sigmoid", [P, 2, BANK])
        z = sb("gated", [P, 2, BANK])
        sq = sb("squares", [P, 2, 4, BANK])
        zero = sb("zero_rows", [P, D])
        zero_set, zero_st = sem("zero_set"), sem("zero_rows_stored")
        ld, yT_psum, yT_done, glu_done, sig_done = (sem(n) for n in ("glu_in", "yT_psum", "yT_done", "glu_done", "sig_done"))
        gated, squared, scaled, sum_done, fin = (sem(n) for n in ("gated", "squared", "scaled", "sum_done", "ssm_rms"))
        with nc.Block() as block:

            @block.gpsimd
            def _(pool):
                pool.memset(zero[:], 0.0).then_inc(zero_set, 1)
                pool.wait_ge(zero_set, 1)
                for b in range(MIN_BLK, NBLK + 2):
                    pool.dma_start(d["rows"][b], zero[:]).then_inc(zero_st, 16)
                pool.wait_ge(zero_st, 16 * (NBLK + 2 - MIN_BLK))

            @block.sync
            def _(sp):
                sp.dma_start(wg[:], a["w_glu"][0].rearrange("(k p) n -> p k n", p=P)).then_inc(ld, 16)
                sp.dma_start(bg[:], a["b_glu"][0].rearrange("(k p) -> p k", p=P), allow_slow_non_contiguous=True).then_inc(ld, 16)
                sp.dma_start(gg[:], a["ssm_norm"][0].rearrange("(k p) -> p k", p=P), allow_slow_non_contiguous=True).then_inc(ld, 16)

            @block.scalar
            def _(act):
                yTv = yT[:].rearrange("p k (h m j) -> p k h m j", h=2, j=CH)
                for n in range(2 * CH):
                    act.wait_ge(yT_psum, n + 1)
                    act.activation(yTv[:, :, n // CH, :, n % CH], bank[n % 4][:].rearrange("p (k m) -> p k m", k=4),
                                   ACT.Copy).then_inc(yT_done, 1)
                act.wait_ge(ld, 48)
                for n in range(16):
                    act.wait_ge(glu_done, n + 1)
                    if n >= 2:
                        act.wait_ge(gated, n - 1)
                    act.activation(sg[:, n % 2], bank[4 + n % 3][:], ACT.Sigmoid, bias=bg[:, n % 4:n % 4 + 1]).then_inc(sig_done, 1)
                act.wait_ge(fin, 1)
                act.activation(srs[:], srs[:], ACT.Sqrt).then_inc(fin, 1)

            @block.vector
            def _(dve):
                for n in range(16):
                    t, oc = n // 4, n % 4
                    cols = slice(t * BANK, (t + 1) * BANK)
                    dve.wait_ge(sig_done, n + 1)
                    if n >= 2:
                        dve.wait_ge(scaled, n - 1)
                        dve.wait_ge(squared, n - 1)
                    dve.tensor_tensor(z[:, n % 2], yT[:, oc, cols], sg[:, n % 2], ALU.mult).then_inc(gated, 1)
                    dve.wait_ge(gated, n + 1)
                    if t >= 2:
                        dve.wait_ge(sum_done, t - 1)
                    dve.tensor_tensor(sq[:, t % 2, oc], z[:, n % 2], z[:, n % 2], ALU.mult).then_inc(squared, 1)
                    dve.tensor_scalar(ssmT[:, oc, cols], z[:, n % 2], gg[:, oc:oc + 1], None, ALU.mult).then_inc(scaled, 1)
                dve.wait_ge(sum_done, 4)
                dve.tensor_scalar(srs[:], bank[7][:, 0:NT], 1.0 / SW, EPS, ALU.mult, ALU.add).then_inc(fin, 1)
                dve.wait_ge(fin, 2)
                dve.reciprocal(srs[:], srs[:]).then_inc(fin, 1)
                dve.wait_ge(fin, 3)

            @block.tensor
            def _(pe):
                for n in range(2 * CH):
                    if n >= 4:
                        pe.wait_ge(yT_done, n - 3)
                    for k in range(4):
                        last = pe.transpose(bank[n % 4][:, k * P:(k + 1) * P], Y[:, n // CH, n % CH, k * P:(k + 1) * P], ident[:])
                    last.then_inc(yT_psum, 1)
                pe.wait_ge(yT_done, 2 * CH)
                pe.wait_ge(ld, 48)

                def sums(t):
                    pe.wait_ge(squared, 4 * (t + 1))
                    for i in range(4):
                        for k in range(4):
                            last = pe.matmul(bank[7][:, 4 * t + i:4 * t + i + 1], sq[:, t % 2, k, i * P:(i + 1) * P], ones[:, 0:1],
                                             start=k == 0, stop=k == 3)
                    last.then_inc(sum_done, 1)

                for n in range(16):
                    t, oc = n // 4, n % 4
                    if n >= 3:
                        pe.wait_ge(sig_done, n - 2)
                    for k in range(4):
                        last = pe.matmul(bank[4 + n % 3][:], wg[:, k, oc * P:(oc + 1) * P], yT[:, k, t * BANK:(t + 1) * BANK],
                                         start=k == 0, stop=k == 3)
                    last.then_inc(glu_done, 1)
                    if n % 4 == 1 and t:
                        sums(t - 1)
                sums(3)


def attention(nc, ident, oT, a, d):
    UN = HEADS * NT
    SLOTS = 3
    slopes = [2.0 ** (-8.0 * (h + 1) / HEADS) for h in range(HEADS)]
    GRP = 4
    width = lambda u: (u % NT + 1) * P
    chunks_of = lambda u: (u % NT + 1 + GRP - 1) // GRP
    qk_before = [0]
    tr_before = [0]
    for u in range(UN):
        qk_before.append(qk_before[-1] + 2 * chunks_of(u))
        tr_before.append(tr_before[-1] + chunks_of(u))
    FIN_AT = [(h + 1) * NT + 4 for h in range(HEADS - 1)]
    with ExitStack() as ctx:
        sb = lambda name, shape, dt=F32: ctx.enter_context(nc.sbuf_tensor(name, shape, dt))
        sem = ctx.enter_context(phase_semaphores(nc))
        bank = [ctx.enter_context(nc.psum_tensor(f"c_bank{i}", [P, BANK], F32)) for i in range(8)]
        q, k = sb("q_head", [P, 2, SEQ]), sb("k_head", [P, 2, SEQ])
        v = sb("v_head", [P, 2, NT, VD])
        bias = sb("alibi", [P, 2, SEQ])
        S = sb("scores", [P, SLOTS, 2, SEQ])
        mx, nm, rs = sb("max_part", [P, SLOTS, 2, 4]), sb("neg_max", [P, SLOTS, 2]), sb("row_sum", [P, SLOTS, 2])
        ri, c2 = sb("row_inv", [P, SLOTS, 2]), sb("map2_scale", [P, SLOTS, 1])
        aT = sb("map_T", [P, 2, BANK])
        o = sb("o_head", [P, 2, NT, VD])
        sqj, oss = sb("o_sq", [P, VD]), sb("o_sumsq", [P, 2, NT])
        lv, lj = sb("lam_vecs", [P, 4, HD]), sb("lam_prod", [P, HD])
        ls = sb("lam_small", [P, 6, 2])
        lsi = sb("lam_int", [P, 2], I32)
        gain = sb("subln", [P, 1])
        qk_in = [sem(f"qkv_in{i}") for i in range(2)]
        lam_in, lam_step, bias_step, bias_ready, gain_ready = (sem(n) for n in ("lam_in", "lam_step", "bias_step", "bias_ready", "gain_ready"))
        qk_done, scored, maxed, exped, inv_step, scaled2, mixed = (
            sem(n) for n in ("qk_done", "scored", "maxed", "exped", "inv_step", "scaled2", "mixed"))
        mapT, aT_ready, pv_chunk, o_used, o_sq = (sem(n) for n in ("mapT", "aT_ready", "pv_chunk", "o_used", "o_sq"))
        fin_dve, fin_act, fin_T, fin_out = (sem(n) for n in ("fin_dve", "fin_act", "fin_T", "fin_out"))
        with nc.Block() as block:

            @block.sync
            def _(sp):
                for h in range(HEADS):
                    if h >= 2:
                        sp.wait_ge(pv_chunk, tr_before[NT * (h - 1)])
                    sp.dma_start(q[:, h % 2], d["qT"][h]).then_inc(qk_in[h % 2], 16)
                    sp.dma_start(k[:, h % 2], d["kT"][h]).then_inc(qk_in[h % 2], 16)
                    sp.dma_start(v[:, h % 2], d["v"].rearrange("(t p) c -> p t c", p=P)[:, :, h * VD:(h + 1) * VD]
                                 ).then_inc(qk_in[h % 2], 16)
                    if h == 0:
                        for n, name in enumerate(("lambda_q1", "lambda_k1", "lambda_q2", "lambda_k2")):
                            sp.dma_start(lv[:, n], a[name].to_broadcast([P, HD])).then_inc(lam_in, 16)
                        sp.dma_start(gain[:], a["attn_subln"].rearrange("l (v o) -> (l v) o", o=1)).then_inc(lam_in, 16)

            @block.gpsimd
            def _(pool):
                def make_bias(h):
                    if h >= 2:
                        pool.wait_ge(scored, qk_before[NT * (h - 1)])
                    t, ti = bias[:, h % 2], bias[:, h % 2].bitcast(I32)
                    pool.iota(ti, pattern=[[1, SEQ]], base=-(SEQ - P), channel_multiplier=-1).then_inc(bias_step, 1)
                    pool.wait_ge(bias_step, 3 * h + 1)
                    pool.tensor_copy(t, ti).then_inc(bias_step, 1)
                    pool.wait_ge(bias_step, 3 * h + 2)
                    pool.tensor_scalar(t, t, slopes[h], None, ALU.mult).then_inc(bias_step, 1)
                    pool.wait_ge(bias_step, 3 * h + 3)
                    pool.affine_select(out=t, in_=t, pattern=[[-1, SEQ]], compare_op=ALU.is_ge,
                                       fill=-BIG, base=SEQ - P, channel_multiplier=1).then_inc(bias_ready, 1)

                make_bias(0)
                make_bias(1)
                for u in range(UN):
                    if u in (NT + 1, 2 * NT + 1):
                        make_bias(u // NT + 1)
                    pool.wait_ge(inv_step, 2 * (u + 1))
                    L = width(u)
                    pool.tensor_scalar(S[:, u % SLOTS, 1, 0:L], S[:, u % SLOTS, 1, 0:L], c2[:, u % SLOTS, 0:1], None,
                                       ALU.mult).then_inc(scaled2, 1)

            @block.vector
            def _(dve):
                dve.wait_ge(lam_in, 80)
                step = Step(dve, lam_step)
                for m in range(2):
                    step(dve.tensor_tensor(lj[:], lv[:, 2 * m], lv[:, 2 * m + 1], ALU.mult))
                    step(dve.tensor_reduce(ls[:, 0, m:m + 1], lj[:], AX.X, ALU.add))
                exact_exp(step, dve, ls[:, 1], ls[:, 0], ls[:, 2], ls[:, 3], lsi[:])
                step(dve.tensor_scalar(ls[:, 4, 0:1], ls[:, 1, 0:1], LAM_INIT, None, ALU.add))
                step(dve.tensor_tensor(ls[:, 5, 0:1], ls[:, 1, 1:2], ls[:, 4, 0:1], ALU.subtract))
                dve.tensor_scalar(gain[:], gain[:], 1.0 - LAM_INIT, None, ALU.mult).then_inc(gain_ready, 1)

                def score(u):
                    h, i, s = u // NT, u % NT, u % SLOTS
                    if i == 0:
                        dve.wait_ge(bias_ready, h + 1)
                    if u >= SLOTS:
                        dve.wait_ge(mapT, tr_before[u - SLOTS + 1])
                    L, n, nch = width(u), qk_before[u], chunks_of(u)
                    for m in range(2):
                        for c in range(nch):
                            w = min(BANK, L - c * BANK)
                            dve.wait_ge(qk_done, n + 1)
                            x0 = c * BANK + SEQ - P - P * i
                            dve.tensor_tensor_reduce(S[:, s, m, c * BANK:c * BANK + w], bank[n % 4][:, 0:w],
                                                     bias[:, h % 2, x0:x0 + w], 1.0, -BIG, ALU.add, ALU.max,
                                                     mx[:, s, m, c:c + 1]).then_inc(scored, 1)
                            n += 1
                    dve.wait_ge(scored, n)
                    dve.tensor_reduce(nm[:, s], mx[:, s, :, 0:nch], AX.X, ALU.max, negate=True).then_inc(maxed, 1)

                def mix(u):
                    s, L = u % SLOTS, width(u)
                    dve.wait_ge(exped, 2 * (u + 1))
                    dve.reciprocal(ri[:, s], rs[:, s]).then_inc(inv_step, 1)
                    dve.wait_ge(inv_step, 2 * u + 1)
                    dve.tensor_tensor(c2[:, s], ri[:, s, 1:2], ls[:, 5, 0:1], ALU.mult).then_inc(inv_step, 1)
                    dve.wait_ge(scaled2, u + 1)
                    dve.scalar_tensor_tensor(S[:, s, 0, 0:L], S[:, s, 0, 0:L], ri[:, s, 0:1], S[:, s, 1, 0:L],
                                             ALU.mult, ALU.add).then_inc(mixed, 1)

                def norm(h):
                    dve.wait_ge(o_sq, NT * (h + 1))
                    dve.tensor_scalar(oss[:, h % 2], oss[:, h % 2], 1.0 / VD, EPS, ALU.mult, ALU.add).then_inc(fin_dve, 1)
                    dve.wait_ge(fin_act, h + 1)
                    dve.reciprocal(oss[:, h % 2], oss[:, h % 2]).then_inc(fin_dve, 1)
                    dve.wait_ge(fin_dve, 3 * h + 2)
                    r = oss[:, h % 2].rearrange("p (t o) -> p t o", o=1).to_broadcast([P, NT, VD])
                    dve.tensor_tensor(o[:, h % 2], o[:, h % 2], r, ALU.mult).then_inc(fin_dve, 1)

                for n in range(UN + 1):
                    if n < UN:
                        score(n)
                    if n >= 1:
                        mix(n - 1)
                    if n in FIN_AT:
                        norm(FIN_AT.index(n))
                norm(HEADS - 1)

            @block.scalar
            def _(act):
                def exps(u):
                    s, L = u % SLOTS, width(u)
                    act.wait_ge(maxed, u + 1)
                    for m in range(2):
                        act.activation(S[:, s, m, 0:L], S[:, s, m, 0:L], ACT.Exp, bias=nm[:, s, m:m + 1],
                                       accum_out=rs[:, s, m:m + 1]).then_inc(exped, 1)

                def evacuate(u):
                    h, i = u // NT, u % NT
                    for c in range(chunks_of(u)):
                        n = tr_before[u] + c
                        w = min(BANK, width(u) - c * BANK)
                        act.wait_ge(mapT, n + 1)
                        if n >= 2:
                            act.wait_ge(pv_chunk, n - 1)
                        act.activation(aT[:, n % 2, 0:w], bank[4 + n % 2][:, 0:w], ACT.Copy).then_inc(aT_ready, 1)
                    act.wait_ge(pv_chunk, tr_before[u + 1])
                    if i == 0 and h >= 2:
                        act.wait_ge(fin_T, 4 * (h - 1))
                    act.activation(o[:, h % 2, i], bank[6 + u % 2][:, 0:VD], ACT.Copy).then_inc(o_used, 1)
                    if u:
                        act.wait_ge(o_sq, u)
                    act.activation(sqj[:], bank[6 + u % 2][:, 0:VD], ACT.Square, accum_out=oss[:, h % 2, i:i + 1]).then_inc(o_sq, 1)

                def finish(h):
                    act.wait_ge(fin_dve, 3 * h + 1)
                    act.activation(oss[:, h % 2], oss[:, h % 2], ACT.Sqrt).then_inc(fin_act, 1)
                    act.wait_ge(gain_ready, 1)
                    for t in range(4):
                        act.wait_ge(fin_T, 4 * h + t + 1)
                        act.activation(oT[:, h, t * BANK:(t + 1) * BANK], bank[4 + t % 2][:], ACT.Copy,
                                       scale=gain[:, 0:1]).then_inc(fin_out, 1)

                for n in range(UN + 2):
                    if 1 <= n <= UN:
                        exps(n - 1)
                    if n >= 2:
                        evacuate(n - 2)
                    if n in FIN_AT:
                        finish(FIN_AT.index(n))
                finish(HEADS - 1)

            @block.tensor
            def _(pe):
                def qk(u):
                    h, i = u // NT, u % NT
                    if i == 0:
                        pe.wait_ge(qk_in[h % 2], 48 * (h // 2 + 1))
                    n = qk_before[u]
                    for m in range(2):
                        half = slice(m * HD, (m + 1) * HD)
                        for c in range(chunks_of(u)):
                            w = min(BANK, width(u) - c * BANK)
                            if n >= 4:
                                pe.wait_ge(scored, n - 3)
                            pe.matmul(bank[n % 4][:, 0:w], q[half, h % 2, i * P:(i + 1) * P], k[half, h % 2, c * BANK:c * BANK + w],
                                      start=True, stop=True).then_inc(qk_done, 1)
                            n += 1

                def pv(u, c):
                    h, n = u // NT, tr_before[u] + c
                    w = min(BANK, width(u) - c * BANK) // P
                    pe.wait_ge(aT_ready, n + 1)
                    if c == 0 and u >= 2:
                        pe.wait_ge(o_used, u - 1)
                        pe.wait_ge(o_sq, u - 1)
                    for b in range(w):
                        kt = GRP * c + b
                        last = pe.matmul(bank[6 + u % 2][:, 0:VD], aT[:, n % 2, b * P:(b + 1) * P], v[:, h % 2, kt],
                                         start=kt == 0, stop=kt == u % NT)
                    last.then_inc(pv_chunk, 1)

                def transpose_and_multiply(u):
                    pe.wait_ge(mixed, u + 1)
                    for c in range(chunks_of(u)):
                        n = tr_before[u] + c
                        if n >= 2:
                            pe.wait_ge(aT_ready, n - 1)
                        w = min(BANK, width(u) - c * BANK) // P
                        for b in range(w):
                            last = pe.transpose(bank[4 + n % 2][:, b * P:(b + 1) * P],
                                                S[:, u % SLOTS, 0, c * BANK + b * P:c * BANK + (b + 1) * P], ident[:])
                        last.then_inc(mapT, 1)
                        if c:
                            pv(u, c - 1)
                    pv(u, chunks_of(u) - 1)

                def head_T(h):
                    pe.wait_ge(fin_dve, 3 * (h + 1))
                    for t in range(4):
                        if t >= 2:
                            pe.wait_ge(fin_out, 4 * h + t - 1)
                        for b in range(4):
                            last = pe.transpose(bank[4 + t % 2][:, b * P:(b + 1) * P], o[:, h % 2, 4 * t + b], ident[:])
                        last.then_inc(fin_T, 1)
                    pe.wait_ge(fin_out, 4 * h + 4)

                for n in range(UN + 2):
                    if n < UN:
                        qk(n)
                    if n >= 2:
                        transpose_and_multiply(n - 2)
                    if n in FIN_AT:
                        head_T(FIN_AT.index(n))
                head_T(HEADS - 1)


def out_projection(nc, ident, oT, ssmT, srs, logits, a, d):
    W = NEG + NE
    with ExitStack() as ctx:
        sb = lambda name, shape, dt=F32: ctx.enter_context(nc.sbuf_tensor(name, shape, dt))
        sem = ctx.enter_context(phase_semaphores(nc))
        bank = [ctx.enter_context(nc.psum_tensor(f"d_bank{i}", [P, BANK], F32)) for i in range(8)]
        wo = sb("w_out", [P, KT, D])
        wr = sb("w_router", [P, KT, W])
        br = sb("b_router", [P, W])
        gain = sb("gain_moe", [P, D])
        x = sb("x_again", [P, 2, D])
        x1, h2 = sb("x1_tile", [P, 2, D]), sb("h2_tile", [P, 2, D])
        tmp = sb("x1_tmp", [P, 2, BANK])
        junk = sb("junk_d", [P, D])
        ss = sb("sumsq_d", [P, NT])
        h2T = sb("h2T", [P, KT, P])
        wo_in, wr_in, gain_in = sem("w_out_in"), sem("w_router_in"), sem("gain_moe_in")
        x_in = [sem(f"x_again_in{i}") for i in range(2)]
        mm_done, tmp_done, x1_done, sq_done, rstd_step, root, h2_done = (
            sem(n) for n in ("wo_done", "tmp_done", "x1_done", "x1_sq", "rstd_d", "root_d", "h2_done"))
        h2T_psum, h2T_done, lg_done, lg_used = (sem(n) for n in ("h2T_psum", "h2T_done", "lg_done", "lg_used"))
        x1_st = [sem(f"x1_stored{i}") for i in range(2)]
        h2_st = [sem(f"h2_stored{i}") for i in range(2)]
        with nc.Block() as block:

            @block.sync
            def _(sp):
                for c in range(2):
                    sp.dma_start(wo[:, :, c * BANK:(c + 1) * BANK],
                                 a["w_out"][0].rearrange("(k p) n -> p k n", p=P)[:, :, c * BANK:(c + 1) * BANK]).then_inc(wo_in, 16)
                sp.dma_start(gain[:], a["norm_moe"].to_broadcast([P, D])).then_inc(gain_in, 16)
                sp.dma_start(wr[:, :, 0:NEG], a["w_router_group"][0].rearrange("(p k) n -> p k n", k=KT)).then_inc(wr_in, 16)
                sp.dma_start(wr[:, :, NEG:W], a["w_router_expert"][0].rearrange("(p k) n -> p k n", k=KT)).then_inc(wr_in, 16)
                sp.dma_start(br[:, 0:NEG], a["b_router_group"].to_broadcast([P, NEG])).then_inc(wr_in, 16)
                sp.dma_start(br[:, NEG:W], a["b_router_expert"].to_broadcast([P, NE])).then_inc(wr_in, 16)
                for i in range(NT + 1):
                    if i < NT:
                        if i >= 2:
                            sp.wait_ge(tmp_done, 2 * (i - 1))
                        sp.dma_start(x[:, i % 2], a["x"][0, i * P:(i + 1) * P]).then_inc(x_in[i % 2], 16)
                    if i:
                        t = i - 1
                        sp.wait_ge(x1_done, 2 * (t + 1))
                        sp.dma_start(d["x1"][t * P:(t + 1) * P], x1[:, t % 2]).then_inc(x1_st[t % 2], 16)
                        sp.wait_ge(h2_done, t + 1)
                        sp.dma_start(d["h2"][t * P:(t + 1) * P], h2[:, t % 2]).then_inc(h2_st[t % 2], 16)
                for s in range(2):
                    sp.wait_ge(x1_st[s], 16 * NT // 2)
                    sp.wait_ge(h2_st[s], 16 * NT // 2)

            @block.scalar
            def _(act):
                def h2_out(t):
                    for h in range(2):
                        act.wait_ge(h2T_psum, 2 * t + h + 1)
                        if t and h == 0:
                            act.wait_ge(lg_done, t)
                        act.activation(h2T[:, 4 * h:4 * h + 4], bank[4 + h][:].rearrange("p (k t) -> p k t", k=4), ACT.Copy
                                       ).then_inc(h2T_done, 1)
                for i in range(NT):
                    act.wait_ge(x1_done, 2 * (i + 1))
                    if i:
                        act.wait_ge(sq_done, i)
                    act.activation(junk[:], x1[:, i % 2], ACT.Square, accum_out=ss[:, i:i + 1]).then_inc(sq_done, 1)
                    act.wait_ge(rstd_step, 2 * i + 1)
                    act.activation(ss[:, i:i + 1], ss[:, i:i + 1], ACT.Sqrt).then_inc(root, 1)
                    h2_out(i)

            @block.vector
            def _(dve):
                def router(t):
                    dve.wait_ge(lg_done, t + 1)
                    dve.tensor_tensor(logits[:, t], bank[6 + t % 2][:, 0:W], br[:], ALU.add).then_inc(lg_used, 1)
                dve.wait_ge(gain_in, 16)
                dve.wait_ge(wr_in, 64)
                for i in range(NT):
                    dve.wait_ge(x_in[i % 2], 16 * (i // 2 + 1))
                    if i >= 2:
                        dve.wait_ge(x1_st[i % 2], 16 * (i // 2))
                    for h in range(2):
                        cols = slice(h * BANK, (h + 1) * BANK)
                        dve.wait_ge(mm_done, 2 * i + h + 1)
                        if 2 * i + h >= 2:
                            dve.wait_ge(x1_done, 2 * i + h - 1)
                        dve.scalar_tensor_tensor(tmp[:, h], bank[2 * h + 1][:], srs[:, i:i + 1], x[:, i % 2, cols],
                                                 ALU.mult, ALU.add).then_inc(tmp_done, 1)
                        dve.wait_ge(tmp_done, 2 * i + h + 1)
                        dve.tensor_tensor(x1[:, i % 2, cols], bank[2 * h][:], tmp[:, h], ALU.add).then_inc(x1_done, 1)
                    dve.wait_ge(sq_done, i + 1)
                    dve.tensor_scalar(ss[:, i:i + 1], ss[:, i:i + 1], 1.0 / D, EPS, ALU.mult, ALU.add).then_inc(rstd_step, 1)
                    dve.wait_ge(root, i + 1)
                    dve.reciprocal(ss[:, i:i + 1], ss[:, i:i + 1]).then_inc(rstd_step, 1)
                    dve.wait_ge(rstd_step, 2 * i + 2)
                    if i >= 2:
                        dve.wait_ge(h2_st[i % 2], 16 * (i // 2))
                        dve.wait_ge(h2T_psum, 2 * (i - 1))
                    dve.scalar_tensor_tensor(h2[:, i % 2], x1[:, i % 2], ss[:, i:i + 1], gain[:], ALU.mult, ALU.mult).then_inc(h2_done, 1)
                    if i:
                        router(i - 1)
                router(NT - 1)
                dve.wait_ge(lg_used, NT)

            @block.tensor
            def _(pe):
                def router(t):
                    pe.wait_ge(h2_done, t + 1)
                    for h in range(2):
                        if t:
                            pe.wait_ge(h2T_done, 2 * t + h - 1)
                        for k in range(4):
                            last = pe.transpose(bank[4 + h][:, k * P:(k + 1) * P], h2[:, t % 2, 4 * h + k:D:KT], ident[:])
                        last.then_inc(h2T_psum, 1)
                    pe.wait_ge(h2T_done, 2 * t + 2)
                    if t >= 2:
                        pe.wait_ge(lg_used, t - 1)
                    for k in range(KT):
                        last = pe.matmul(bank[6 + t % 2][:, 0:W], h2T[:, k], wr[:, k], start=k == 0, stop=k == KT - 1)
                    last.then_inc(lg_done, 1)

                pe.wait_ge(wr_in, 64)
                pe.wait_ge(wo_in, 32)
                for i in range(NT):
                    for h in range(2):
                        cols = slice(h * BANK, (h + 1) * BANK)
                        if i:
                            pe.wait_ge(x1_done, 2 * i + h - 1)
                        for k in range(4):
                            pe.matmul(bank[2 * h][:], oT[:, k, i * P:(i + 1) * P], wo[:, k, cols], start=k == 0, stop=k == 3)
                        for k in range(4):
                            last = pe.matmul(bank[2 * h + 1][:], ssmT[:, k, i * P:(i + 1) * P], wo[:, 4 + k, cols], start=k == 0, stop=k == 3)
                        last.then_inc(mm_done, 1)
                    if i:
                        router(i - 1)
                router(NT - 1)


def route(nc, ident, ones, logits, gates, dest, ids, meta, d):
    W = NEG + NE
    with ExitStack() as ctx:
        sb = lambda name, shape, dt=F32: ctx.enter_context(nc.sbuf_tensor(name, shape, dt))
        sem = ctx.enter_context(phase_semaphores(nc))
        bank = [ctx.enter_context(nc.psum_tensor(f"r_bank{i}", [P, BANK], F32)) for i in range(3)]
        count_i, count = sb("count_i", [P, P], I32), sb("count", [P, P])
        tri = sb("earlier", [P, P])
        thr = sb("block_edges", [P, NT])
        tok = sb("token_id", [P, NT], I32)
        zero = sb("zero_ids", [NBLK, P], I32)
        t1 = lambda n: sb(n, [P, NT, 1])
        gmax, gidx, gsum, m1, m2, i1, i2, esum = (t1(n) for n in ("gmax", "gidx", "gsum", "m1", "m2", "i1", "i2", "esum"))
        g_eq, goh, gex = (sb(n, [P, NT, NEG]) for n in ("g_eq", "g_onehot", "g_exp"))
        ein, etmp, oh1, oh2, eex = (sb(n, [P, NT, EPG]) for n in ("e_in", "e_tmp", "onehot1", "onehot2", "e_exp"))
        p2 = t1("p2")
        A = sb("assigned", [P, 2, NT, NEG, EPG])
        M = sb("assigned_any", [P, NT, NE])
        base = sb("rank_base", [P, NT + 1, NE])
        big = sb("compare", [P, NBLK, NE])
        nblk, pend, sbase, rank = sb("n_blocks", [P, NE]), sb("block_end", [P, NE]), sb("slot_base", [P, NE]), sb("rank", [P, NT, NE])
        df, bf = sb("dest_f", [P, NT, 1]), sb("meta_f", [P, NBLK + 2])
        idf = sb("ids_f", [NBLK, P])
        idi = sb("ids_i", [NBLK, P], I32)
        c_step, c_ready, r_step, exp_in, exp_done, any_ready, pref_done = (
            sem(n) for n in ("c_step", "c_ready", "r_step", "exp_in", "exp_done", "any_ready", "pref_done"))
        zero_st, dest_ready, scattered, ids_in, ids_f, ids_T = (
            sem(n) for n in ("zero_stored", "dest_ready", "scattered", "ids_loaded", "ids_f_ready", "ids_T"))
        with nc.Block() as block:

            @block.gpsimd
            def _(pool):
                pool.iota(count_i[:], pattern=[[1, P]], base=0, channel_multiplier=0).then_inc(c_step, 1)
                pool.iota(tok[:], pattern=[[P, NT]], base=0, channel_multiplier=1).then_inc(c_step, 1)
                pool.memset(zero[:], 0).then_inc(c_step, 1)
                pool.memset(ids[:], 0).then_inc(c_step, 1)
                pool.wait_ge(c_step, 4)
                pool.tensor_copy(count[:], count_i[:]).then_inc(c_step, 1)
                pool.wait_ge(c_step, 5)
                pool.tensor_scalar(thr[:], count[:, 0:NT], float(P), None, ALU.mult).then_inc(c_ready, 1)
                pool.affine_select(out=tri[:], in_=ones[:], pattern=[[1, P]], compare_op=ALU.is_gt, fill=0.0,
                                   base=0, channel_multiplier=-1).then_inc(c_ready, 1)
                pool.wait_ge(zero_st, 16)
                pool.wait_ge(dest_ready, 2)
                for k in range(2):
                    for i in range(NT):
                        pool.indirect_dma_start(d["slot_token"], bass.IndirectOffsetOnAxis(ap=dest[:, k, i:i + 1], axis=0),
                                                tok[:, i:i + 1], None).then_inc(scattered, 16)
                pool.wait_ge(scattered, 16 * 2 * NT)

            @block.sync
            def _(sp):
                sp.wait_ge(c_step, 3)
                sp.dma_start(d["slot_token"].rearrange("(b p) o -> b (p o)", p=P), zero[:]).then_inc(zero_st, 16)
                sp.wait_ge(scattered, 16 * 2 * NT)
                sp.dma_start(idi[:], d["slot_token"].rearrange("(b p) o -> b (p o)", p=P)).then_inc(ids_in, 16)

            @block.scalar
            def _(act):
                act.wait_ge(exp_in, 1)
                act.activation(gex[:], gex[:], ACT.Exp).then_inc(exp_done, 1)
                act.wait_ge(exp_in, 3)
                act.activation(eex[:], eex[:], ACT.Exp).then_inc(exp_done, 1)
                act.activation(p2[:], p2[:], ACT.Exp).then_inc(exp_done, 1)

            @block.tensor
            def _(pe):
                pe.wait_ge(c_ready, 2)
                pe.wait_ge(any_ready, 1)
                m = M[:].rearrange("p t e -> p (t e)")
                pe.matmul(bank[0][:], tri[:], m, start=True, stop=True)
                pe.matmul(bank[1][:], ones[:], m, start=True, stop=True).then_inc(pref_done, 1)
                pe.wait_ge(ids_f, 1)
                pe.transpose(bank[2][:, 0:NBLK], idf[:], ident[0:NBLK, 0:NBLK]).then_inc(ids_T, 1)

            @block.vector
            def _(dve):
                step = Step(dve, r_step)
                Lg, Le = logits[:, :, 0:NEG], logits[:, :, NEG:W]
                wide = lambda t, n: t.to_broadcast([P, NT, n])
                dve.wait_ge(c_ready, 2)

                def first_max(val, n, mxt, idx, out, tmp):
                    step(dve.tensor_reduce(mxt[:], val, AX.X, ALU.max))
                    step(dve.tensor_tensor(tmp[:], val, wide(mxt[:], n), ALU.is_ge))
                    cnt = count[:, 0:n].rearrange("p (o n) -> p o n", o=1).to_broadcast([P, NT, n])
                    step(dve.scalar_tensor_tensor(tmp[:], tmp[:], -64.0, cnt, ALU.mult, ALU.add))
                    step(dve.tensor_reduce(idx[:], tmp[:], AX.X, ALU.min))
                    step(dve.tensor_tensor(out[:], tmp[:], wide(idx[:], n), ALU.is_equal))

                first_max(Lg, NEG, gmax, gidx, goh, g_eq)
                dve.tensor_tensor(gex[:], Lg, wide(gmax[:], NEG), ALU.subtract).then_inc(exp_in, 1)
                for g in range(NEG):
                    o = wide(goh[:, :, g:g + 1], EPG)
                    e = Le[:, :, g * EPG:(g + 1) * EPG]
                    if g == 0:
                        step(dve.tensor_tensor(ein[:], e, o, ALU.mult))
                    else:
                        step(dve.tensor_tensor(etmp[:], e, o, ALU.mult))
                        step(dve.tensor_tensor(ein[:], ein[:], etmp[:], ALU.add))
                first_max(ein[:], EPG, m1, i1, oh1, etmp)
                dve.tensor_tensor(eex[:], ein[:], wide(m1[:], EPG), ALU.subtract).then_inc(exp_in, 1)
                dve.wait_ge(exp_in, 2)
                step(dve.scalar_tensor_tensor(ein[:], oh1[:], -BIG, ein[:], ALU.mult, ALU.add))
                first_max(ein[:], EPG, m2, i2, oh2, etmp)
                dve.tensor_tensor(p2[:], m2[:], m1[:], ALU.subtract).then_inc(exp_in, 1)
                for k, oh in enumerate((oh1, oh2)):
                    g4 = goh[:].rearrange("p t (g o) -> p t g o", o=1).to_broadcast([P, NT, NEG, EPG])
                    e4 = oh[:].rearrange("p t (o e) -> p t o e", o=1).to_broadcast([P, NT, NEG, EPG])
                    step(dve.tensor_tensor(A[:, k], g4, e4, ALU.mult))
                Ak = [A[:, k].rearrange("p t g e -> p t (g e)") for k in range(2)]
                dve.tensor_tensor(M[:], Ak[0], Ak[1], ALU.add).then_inc(any_ready, 1)
                dve.wait_ge(exp_done, 3)
                step(dve.tensor_reduce(gsum[:], gex[:], AX.X, ALU.add))
                step(dve.tensor_reduce(esum[:], eex[:], AX.X, ALU.add))
                step(dve.tensor_tensor(gsum[:], gsum[:], esum[:], ALU.mult))
                step(dve.reciprocal(gates[:, 0], gsum[:, :, 0]))
                step(dve.tensor_tensor(gates[:, 1], gates[:, 0], p2[:, :, 0], ALU.mult))
                dve.wait_ge(pref_done, 1)
                tot = bank[1][:].rearrange("p (t e) -> p t e", e=NE)
                step(dve.memset(base[:, 0], 0.0))
                for i in range(NT):
                    step(dve.tensor_tensor(base[:, i + 1], base[:, i], tot[:, i], ALU.add))
                cmp1 = big[:].rearrange("p b e -> p (b e)")[:, 0:NE * NT].rearrange("p (e j) -> p e j", j=NT)
                step(dve.tensor_tensor(cmp1, base[:, NT].rearrange("p (e o) -> p e o", o=1).to_broadcast([P, NE, NT]),
                                       thr[:].rearrange("p (o j) -> p o j", o=1).to_broadcast([P, NE, NT]), ALU.is_gt))
                step(dve.tensor_reduce(nblk[:], cmp1, AX.X, ALU.add))
                step(dve.tensor_tensor_scan(pend[:], ones[:, 0:NE], nblk[:], 0.0, ALU.mult, ALU.add))
                step(dve.tensor_tensor(sbase[:], pend[:], nblk[:], ALU.subtract))
                step(dve.tensor_scalar(sbase[:], sbase[:], float(P), None, ALU.mult))
                step(dve.tensor_tensor(rank[:], base[:, 0:NT], bank[0][:].rearrange("p (t e) -> p t e", e=NE), ALU.add))
                step(dve.tensor_tensor(rank[:], rank[:], sbase[:].rearrange("p (o e) -> p o e", o=1).to_broadcast([P, NT, NE]), ALU.add))
                for k in range(2):
                    step(dve.tensor_tensor(M[:], Ak[k], rank[:], ALU.mult))
                    step(dve.tensor_reduce(df[:], M[:], AX.X, ALU.add))
                    dve.tensor_copy(dest[:, k], df[:, :, 0]).then_inc(dest_ready, 1)
                    dve.wait_ge(dest_ready, k + 1)
                step(dve.tensor_tensor(big[:], pend[:].rearrange("p (o e) -> p o e", o=1).to_broadcast([P, NBLK, NE]),
                                       count[:, 0:NBLK].rearrange("p (b o) -> p b o", o=1).to_broadcast([P, NBLK, NE]), ALU.is_le))
                step(dve.tensor_reduce(bf[:, 0:NBLK], big[:], AX.X, ALU.add))
                step(dve.tensor_scalar(bf[:, 0:NBLK], bf[:, 0:NBLK], float(NE - 1), None, ALU.min))
                step(dve.tensor_scalar(bf[:, NBLK:NBLK + 1], pend[:, NE - 1:NE], 1.0, None, ALU.add))
                step(dve.tensor_copy(meta[:, 0:NBLK + 1], bf[:, 0:NBLK + 1]))
                step(dve.tensor_scalar(meta[:, NBLK:NBLK + 1], meta[:, NBLK:NBLK + 1], 1, None, ALU.logical_shift_right))
                dve.wait_ge(ids_in, 16)
                dve.tensor_copy(idf[:], idi[:]).then_inc(ids_f, 1)
                dve.wait_ge(ids_T, 1)
                step(dve.tensor_copy(ids[:, 0:NBLK], bank[2][:, 0:NBLK]))


def experts(nc, ident, ones, ids, meta, a, d):
    with ExitStack() as ctx:
        sb = lambda name, shape, dt=F32: ctx.enter_context(nc.sbuf_tensor(name, shape, dt))
        sem = ctx.enter_context(phase_semaphores(nc))
        bank = [ctx.enter_context(nc.psum_tensor(f"m_bank{i}", [P, BANK], F32)) for i in range(7)]
        G, U, XT, HT, DN = bank[0], bank[1], bank[2:4], bank[4], bank[5:7]
        FT = FF // P
        wg, wu = sb("w_gate_blk", [P, 2, KT, FF]), sb("w_up_blk", [P, 2, KT, FF])
        wd = sb("w_down_blk", [P, 2, FT, D])
        idx = sb("idx", [P, 2], I32)
        spare, hold, last_copy = sb("spare", [P, 8]), sb("hold", [P, 1]), sb("last_copy", [P, 1])
        x = sb("rows_in", [P, 2, D])
        xT = sb("rows_T", [P, 2, KT, P])
        sil, hid = sb("silu", [P, FF]), sb("hidden", [P, FF])
        hT = sb("hidden_T", [P, FT, P])
        out = sb("rows_out", [P, 2, D])
        two = lambda name: [sem(f"{name}{i}") for i in range(2)]
        g_in, u_in, d_in, x_in, out_st = two("w_gate_in"), two("w_up_in"), two("w_down_in"), two("rows_in_"), two("rows_stored")
        g_done, u_done, d_done, silu_done, hid_done, idx_set = (sem(n) for n in ("g_done", "u_done", "d_done", "silu_done", "hid_done", "idx_set"))
        xT_psum, xT_done, hT_psum, hT_done, d_used0, d_used1, primed = (
            sem(n) for n in ("rT_psum", "rT_done", "hidT_psum", "hidT_done", "d_used0", "d_used1", "primed"))
        with nc.Block() as block:

            @block.vector
            def _(dve):
                dve.memset(out[:], 0.0).then_inc(primed, 1)
                for n, (s, times) in enumerate(((g_done, 2), (u_done, 2), (d_done, 4), (silu_done, 1), (hid_done, 1),
                                                (hT_done, 1), (d_used0, 1), (d_used1, 1))):
                    dve.memset(spare[:, n:n + 1], 0.0).then_inc(s, times)

            @block.scalar
            def _(act):
                act.wait_ge(primed, 1)
                for s in range(2):
                    act.dma_start(d["rows"][NBLK + s], out[:, s]).then_inc(out_st[s], 16)

        with nc.Block() as block:
            pairs = lambda eng: eng.value_load(meta[0:1, NBLK:NBLK + 1], min_val=1, max_val=NBLK // 2)

            @block.sync
            def _(sp):
                with sp.Fori(0, pairs(sp)) as i:
                    for s in range(2):
                        e = sp.value_load(meta[0:1, bass.ds(2 * i + s, 1)], min_val=0, max_val=NE - 1)
                        sp.wait_ge(g_done, 2 * i + s + 1)
                        sp.dma_start(wg[:, s], a["w_gate"][0, bass.ds(e, 1)].rearrange("o (p k) n -> p (o k) n", k=KT)).then_inc(g_in[s], 16)
                        sp.wait_ge(u_done, 2 * i + s + 1)
                        sp.dma_start(wu[:, s], a["w_up"][0, bass.ds(e, 1)].rearrange("o (p k) n -> p (o k) n", k=KT)).then_inc(u_in[s], 16)
                        sp.wait_ge(d_done, 4 * i + 2 * s + 2)
                        sp.dma_start(wd[:, s], a["w_down"][0, bass.ds(e, 1)].rearrange("o (p k) n -> p (o k) n", k=FT)).then_inc(d_in[s], 16)

            @block.gpsimd
            def _(pool):
                def gather(column, slot):
                    n = pool.tensor_copy(idx[:, slot:slot + 1], ids[:, column])
                    return n

                gather(slice(0, 1), 0).then_inc(idx_set, 1)
                pool.wait_ge(idx_set, 1)
                pool.indirect_dma_start(x[:, 0], None, d["h2"], bass.IndirectOffsetOnAxis(ap=idx[:, 0:1], axis=0)).then_inc(x_in[0], 16)
                with pool.Fori(0, pairs(pool)) as i:
                    for s in range(2):
                        t = 1 - s
                        pool.wait_ge(xT_psum, 4 * i + 2 * s + 2)
                        gather(bass.ds(2 * i + s + 1, 1), t).then_inc(idx_set, 1)
                        pool.wait_ge(idx_set, 2 * i + s + 2)
                        pool.tensor_tensor(hold[:], ones[:, 0:1], ones[:, 1:2], ALU.add)
                        pool.indirect_dma_start(x[:, t], None, d["h2"], bass.IndirectOffsetOnAxis(ap=idx[:, t:t + 1], axis=0)
                                                ).then_inc(x_in[t], 16)

            @block.scalar
            def _(act):
                def rows_T(slot, h, want):
                    act.wait_ge(xT_psum, want)
                    act.activation(xT[:, slot, 4 * h:4 * h + 4], XT[h][:].rearrange("p (k t) -> p k t", k=4), ACT.Copy).then_inc(xT_done, 1)

                rows_T(0, 0, 1)
                rows_T(0, 1, 2)
                with act.Fori(0, pairs(act)) as i:
                    for s in range(2):
                        b = 2 * i + s
                        act.wait_ge(g_done, b + 3)
                        act.wait_ge(hid_done, b + 1)
                        act.activation(sil[:], G[:], ACT.Silu).then_inc(silu_done, 1)
                        rows_T(1 - s, 0, 4 * i + 2 * s + 3)
                        act.wait_ge(hT_psum, b + 1)
                        act.activation(hT[:], HT[:].rearrange("p (k t) -> p k t", k=FT), ACT.Copy).then_inc(hT_done, 1)
                        rows_T(1 - s, 1, 4 * i + 2 * s + 4)
                        act.wait_ge(d_done, 4 * i + 2 * s + 5)
                        act.wait_ge(out_st[s], 16 * i + 16)
                        act.activation(out[:, s, 0:BANK], DN[0][:], ACT.Copy).then_inc(d_used0, 1)
                        act.wait_ge(d_used0, b + 2)
                        act.wait_ge(d_used1, b + 2)
                        act.dma_start(d["rows"][bass.ds(b, 1)].rearrange("o p n -> p (o n)"), out[:, s]).then_inc(out_st[s], 16)
                n = pairs(act)
                for s in range(2):
                    act.wait_ge(out_st[s], 16 * n + 16)
                act.activation(last_copy[:], ones[:, 0:1], ACT.Copy)

            @block.vector
            def _(dve):
                with dve.Fori(0, pairs(dve)) as i:
                    for s in range(2):
                        b = 2 * i + s
                        dve.wait_ge(u_done, b + 3)
                        dve.wait_ge(silu_done, b + 2)
                        dve.tensor_tensor(hid[:], sil[:], U[:], ALU.mult).then_inc(hid_done, 1)
                        dve.wait_ge(d_done, 4 * i + 2 * s + 6)
                        dve.wait_ge(out_st[s], 16 * i + 16)
                        dve.tensor_copy(out[:, s, BANK:D], DN[1][:]).then_inc(d_used1, 1)

            @block.tensor
            def _(pe):
                def rows_T(slot, h):
                    for k in range(4):
                        last = pe.transpose(XT[h][:, k * P:(k + 1) * P], x[:, slot, 4 * h + k:D:KT], ident[:])
                    last.then_inc(xT_psum, 1)

                pe.wait_ge(x_in[0], 16)
                rows_T(0, 0)
                rows_T(0, 1)
                with pe.Fori(0, pairs(pe)) as i:
                    for s in range(2):
                        b = 2 * i + s
                        pe.wait_ge(xT_done, 4 * i + 2 * s + 2)
                        pe.wait_ge(silu_done, b + 1)
                        pe.wait_ge(g_in[s], 16 * i + 16)
                        for k in range(KT):
                            last = pe.matmul(G[:], xT[:, s, k], wg[:, s, k], start=k == 0, stop=k == KT - 1)
                        last.then_inc(g_done, 1)
                        pe.wait_ge(hid_done, b + 1)
                        pe.wait_ge(u_in[s], 16 * i + 16)
                        for k in range(KT):
                            last = pe.matmul(U[:], xT[:, s, k], wu[:, s, k], start=k == 0, stop=k == KT - 1)
                        last.then_inc(u_done, 1)
                        pe.wait_ge(x_in[1 - s], 16 * i + 16 + 16 * s)
                        rows_T(1 - s, 0)
                        pe.wait_ge(hid_done, b + 2)
                        pe.wait_ge(hT_done, b + 1)
                        for k in range(FT):
                            last = pe.transpose(HT[:, k * P:(k + 1) * P], hid[:, k:FF:FT], ident[:])
                        last.then_inc(hT_psum, 1)
                        rows_T(1 - s, 1)
                        pe.wait_ge(hT_done, b + 2)
                        pe.wait_ge(d_in[s], 16 * i + 16)
                        pe.wait_ge(d_used0, b + 1)
                        pe.wait_ge(d_used1, b + 1)
                        for h in range(2):
                            for k in range(FT):
                                last = pe.matmul(DN[h][:], hT[:, k], wd[:, s, k, h * BANK:(h + 1) * BANK], start=k == 0, stop=k == FT - 1)
                            last.then_inc(d_done, 1)


def combine(nc, gates, dest, a, d, out):
    R = 3
    with ExitStack() as ctx:
        sb = lambda name, shape, dt=F32: ctx.enter_context(nc.sbuf_tensor(name, shape, dt))
        sem = ctx.enter_context(phase_semaphores(nc))
        r = sb("expert_rows", [P, R, 2, D])
        x1, y = sb("x1_back", [P, R, D]), sb("y_tile", [P, R, D])
        junk = sb("junk_f", [P, D])
        gain = sb("gain_final", [P, D])
        ss = sb("sumsq_f", [P, NT])
        x_in = [sem(f"x1_back_in{i}") for i in range(R)]
        r_in = [sem(f"expert_rows_in{i}") for i in range(R)]
        st = [sem(f"out_stored{i}") for i in range(R)]
        gain_in, mix0, mix1, sq, rstd_step, root, normed = (
            sem(n) for n in ("gain_final_in", "mix_0", "mix_1", "sq_f", "rstd_f", "root_f", "normed_f"))
        with nc.Block() as block:

            @block.gpsimd
            def _(pool):
                for i in range(NT):
                    if i >= R:
                        pool.wait_ge(mix1, i - R + 1)
                    for k in range(2):
                        pool.indirect_dma_start(r[:, i % R, k], None, d["rows"].rearrange("b p n -> (b p) n"),
                                                bass.IndirectOffsetOnAxis(ap=dest[:, k, i:i + 1], axis=0)).then_inc(r_in[i % R], 16)

            @block.sync
            def _(sp):
                sp.dma_start(gain[:], a["norm_final"].rearrange("(o n) -> o n", o=1).to_broadcast([P, D])).then_inc(gain_in, 16)
                for i in range(NT + 1):
                    if i < NT:
                        if i >= R:
                            sp.wait_ge(mix0, i - R + 1)
                        sp.dma_start(x1[:, i % R], d["x1"][i * P:(i + 1) * P]).then_inc(x_in[i % R], 16)
                    if i:
                        t = i - 1
                        sp.wait_ge(normed, t + 1)
                        sp.dma_start(out[0, t * P:(t + 1) * P], y[:, t % R]).then_inc(st[t % R], 16)
                for s in range(R):
                    sp.wait_ge(st[s], 16 * len(range(s, NT, R)))

            @block.scalar
            def _(act):
                for i in range(NT):
                    act.wait_ge(mix1, i + 1)
                    if i:
                        act.wait_ge(sq, i)
                    act.activation(junk[:], y[:, i % R], ACT.Square, accum_out=ss[:, i:i + 1]).then_inc(sq, 1)
                    act.wait_ge(rstd_step, 2 * i + 1)
                    act.activation(ss[:, i:i + 1], ss[:, i:i + 1], ACT.Sqrt).then_inc(root, 1)

            @block.vector
            def _(dve):
                def mix(i):
                    dve.wait_ge(x_in[i % R], 16 * (i // R + 1))
                    dve.wait_ge(r_in[i % R], 32 * (i // R + 1))
                    if i >= R:
                        dve.wait_ge(st[i % R], 16 * (i // R))
                    dve.scalar_tensor_tensor(y[:, i % R], r[:, i % R, 0], gates[:, 0, i:i + 1], x1[:, i % R], ALU.mult, ALU.add).then_inc(mix0, 1)
                    dve.wait_ge(mix0, i + 1)
                    dve.scalar_tensor_tensor(y[:, i % R], r[:, i % R, 1], gates[:, 1, i:i + 1], y[:, i % R], ALU.mult, ALU.add).then_inc(mix1, 1)

                dve.wait_ge(gain_in, 16)
                mix(0)
                for i in range(NT):
                    if i + 1 < NT:
                        mix(i + 1)
                    dve.wait_ge(sq, i + 1)
                    dve.tensor_scalar(ss[:, i:i + 1], ss[:, i:i + 1], 1.0 / D, EPS, ALU.mult, ALU.add).then_inc(rstd_step, 1)
                    dve.wait_ge(root, i + 1)
                    dve.reciprocal(ss[:, i:i + 1], ss[:, i:i + 1]).then_inc(rstd_step, 1)
                    dve.wait_ge(rstd_step, 2 * i + 2)
                    dve.scalar_tensor_tensor(y[:, i % R], y[:, i % R], ss[:, i:i + 1], gain[:], ALU.mult, ALU.mult).then_inc(normed, 1)


def hybrid_layer(nc, a, out):
    dram = lambda name, shape, dt=F32: nc.dram_tensor(name, shape, dt, kind="Internal").ap()
    d = {
        "u": dram("u_d", [2, CH, P, SW]), "v": dram("v_d", [SEQ, SW]),
        "qT": dram("qT_d", [HEADS, P, SEQ]), "kT": dram("kT_d", [HEADS, P, SEQ]),
        "w1": dram("w1_d", [NB, P, GB, P]), "w2": dram("w2_d", [NB, P, GB, P]),
        "q": dram("q_d", [NB, P, GB, CH, GC]), "q2": dram("q2_d", [NB, P, GB, CH, GC]),
        "cos": dram("cos_d", [NB, P, GB, NCH]), "sin": dram("sin_d", [NB, P, GB, NCH]),
        "slot_token": dram("slot_token_d", [NBLK * P, 1], I32), "rows": dram("rows_d", [NBLK + 2, P, D]),
        "x1": dram("x1_d", [SEQ, D]), "h2": dram("h2_d", [SEQ, D]),
        "taps": dram("taps_d", [CH, GC, NG, GC]),
    }
    with ExitStack() as ctx:
        sem = ctx.enter_context(phase_semaphores(nc))
        ident = ctx.enter_context(nc.sbuf_tensor("ident", [P, P], F32))
        r8 = ctx.enter_context(nc.sbuf_tensor("r8", [P, NG], F32))
        ident_step = sem("ident_step")
        with nc.Block() as block:
            @block.gpsimd
            def _(pool):
                pool.memset(ident[:], 0.0).then_inc(ident_step, 1)
                pool.wait_ge(ident_step, 1)
                pool.affine_select(out=ident[:], in_=ident[:], pattern=[[-1, P]], compare_op=ALU.not_equal, fill=1.0,
                                   base=0, channel_multiplier=1).then_inc(ident_step, 1)
                pool.wait_ge(ident_step, 2)
        ones = ctx.enter_context(nc.sbuf_tensor("ones", [P, P], F32))
        ones_set = sem("ones_set")
        with nc.Block() as block:
            @block.vector
            def _(dve):
                dve.memset(ones[:], 1.0).then_inc(ones_set, 1)
                dve.wait_ge(ones_set, 1)
        norm_project_prepare(nc, ident, r8, a, d)
        ssmT = ctx.enter_context(nc.sbuf_tensor("ssmT", [P, 4, SEQ], F32))
        srs = ctx.enter_context(nc.sbuf_tensor("ssm_rstd", [P, NT], F32))
        with nc.sbuf_tensor("u_tok", [P, 2, CH, SW], F32) as U:
            s5_groups(nc, ident, r8, U, a, d)
            s5_gate(nc, ident, ones, U, ssmT, srs, a, d)
        logits = ctx.enter_context(nc.sbuf_tensor("logits", [P, NT, NEG + NE], F32))
        with nc.sbuf_tensor("attn_T", [P, HEADS, SEQ], F32) as oT:
            attention(nc, ident, oT, a, d)
            out_projection(nc, ident, oT, ssmT, srs, logits, a, d)
        gates = ctx.enter_context(nc.sbuf_tensor("gates", [P, 2, NT], F32))
        dest = ctx.enter_context(nc.sbuf_tensor("dest", [P, 2, NT], I32))
        ids = ctx.enter_context(nc.sbuf_tensor("slot_ids", [P, NBLK + 2], I32))
        meta = ctx.enter_context(nc.sbuf_tensor("block_meta", [P, NBLK + 2], I32))
        route(nc, ident, ones, logits, gates, dest, ids, meta, d)
        experts(nc, ident, ones, ids, meta, a, d)
        combine(nc, gates, dest, a, d, out)



_INS = [
    'x', 'norm_attn', 'w_in', 'lambda_q1', 'lambda_k1', 'lambda_q2', 'lambda_k2', 'attn_subln',
    'ssm_lam_re', 'ssm_lam_im', 'ssm_log_dt', 'ssm_b_re', 'ssm_b_im', 'ssm_c_re', 'ssm_c_im', 'ssm_d',
    'w_glu', 'b_glu', 'ssm_norm', 'w_out', 'norm_moe', 'w_router_group', 'b_router_group', 'w_router_expert',
    'b_router_expert', 'w_gate', 'w_up', 'w_down', 'norm_final',
]
_OUTS = [((1, 2048, 1024), 'float32')]


def kernel(**inputs):
    import numpy as _np
    import concourse.bacc as _bacc
    from concourse import mybir as _mybir
    from concourse.bass_utils import run_bass_kernel_spmd as _run

    nc = _bacc.Bacc("TRN2", target_bir_lowering=False, num_devices=1)
    arrays, aps = {}, {}
    for name in _INS:
        v = _np.ascontiguousarray(inputs[name])
        arrays[f"in_{name}_dram"] = v
        aps[name] = nc.dram_tensor(f"in_{name}_dram", v.shape, _mybir.dt.from_np(v.dtype), kind="ExternalInput").ap()
    shape, dtype = _OUTS[0]
    out = nc.dram_tensor("out_0_dram", shape, _mybir.dt.from_np(_np.dtype(dtype)), kind="ExternalOutput").ap()
    hybrid_layer(nc, aps, out)
    r = _run(nc, [arrays], core_ids=[0])
    return r.results[0]["out_0_dram"]
```

```python
from contextlib import ExitStack, contextmanager
import math

import numpy as np
import concourse.bass as bass
import concourse.mybir as mybir

F32 = mybir.dt.float32
I32 = mybir.dt.int32
F32R = mybir.dt.float32r
ALU = mybir.AluOpType
ACT = mybir.ActivationFunctionType
AX = mybir.AxisListType

P = 128
SEQ = 2048
D = 1024
KT = D // P
NT = SEQ // P
HEADS = 4
HD = 64
VD = 128
SW = 512
NG = 32
GC = 16
NS = 64
CH = 8
NCH = SEQ // CH
GB = 8
NB = NG // GB
BANK = 512
EPS = 1e-6
LAM_INIT = 0.8 - 0.6 * math.exp(-0.3 * 0)
NE = 32
NEG = 4
EPG = 8
FF = 512
NBLK = 64
MIN_BLK = 2 * SEQ // P
BIG = 3.0e38
META_ID = NBLK
META_BLOCKS, META_EXPERTS = NBLK + NE, NBLK + NE + 1
META = NBLK + NE + 2


@contextmanager
def phase_semaphores(nc):
    taken = []

    def sem(name):
        taken.append(nc.alloc_semaphore(name=name))
        return taken[-1]

    yield sem
    nc.clear_and_free_semaphores(taken)
    nc.all_engine_barrier()


@contextmanager
def where_below(nc, eng, low, high):
    name = f"where_below_{nc.next_id()}"
    eng.br_lt(low, high, on_true=name + "_body", on_false=name + "_end")
    with nc.body(name + "_body", valid_engines=[eng.engine]):
        yield
        nc.br(name + "_end", engines=[eng.engine])
    nc.switch_bb(name + "_end")


class Step:

    def __init__(self, eng, sem, start=0):
        self.eng, self.sem, self.n = eng, sem, start

    def __call__(self, ins):
        self.n += 1
        ins.then_inc(self.sem, 1)
        self.eng.wait_ge(self.sem, self.n)


def exact_exp(step, eng, out, x, n, q, ni):
    magic = 12582912.0
    step(eng.tensor_scalar(n, x, 1.4426950408889634, -126.0, ALU.mult, ALU.max))
    step(eng.tensor_scalar(n, n, 127.0, magic, ALU.min, ALU.add))
    step(eng.tensor_scalar(n, n, -magic, None, ALU.add))
    step(eng.scalar_tensor_tensor(x, n, -0.693359375, x, ALU.mult, ALU.add))
    step(eng.scalar_tensor_tensor(x, n, 2.12194440e-4, x, ALU.mult, ALU.add))
    step(eng.tensor_scalar(q, x, 1.0 / 40320, None, ALU.mult))
    for k in range(7, 0, -1):
        step(eng.scalar_tensor_tensor(q, q, 1.0 / math.factorial(k), x, ALU.add, ALU.mult))
    step(eng.tensor_scalar(n, n, 127.0, None, ALU.add))
    step(eng.tensor_copy(ni, n))
    step(eng.tensor_scalar(ni, ni, 23, None, ALU.logical_shift_left))
    step(eng.scalar_tensor_tensor(out, q, 1.0, ni.bitcast(F32), ALU.add, ALU.mult))


def complex_mul(step, eng, orr, oi, ar, ai, br, bi, t):
    step(eng.tensor_tensor(orr, ar, br, ALU.mult))
    step(eng.tensor_tensor(t, ai, bi, ALU.mult))
    step(eng.tensor_tensor(orr, orr, t, ALU.subtract))
    step(eng.tensor_tensor(oi, ar, bi, ALU.mult))
    step(eng.tensor_tensor(t, ai, br, ALU.mult))
    step(eng.tensor_tensor(oi, oi, t, ALU.add))


def norm_project_prepare(nc, ident, r8, a, d):
    chunks = [3, 0, 1, 2]
    with ExitStack() as ctx:
        sb = lambda name, shape, dt=F32: ctx.enter_context(nc.sbuf_tensor(name, shape, dt))
        sem = ctx.enter_context(phase_semaphores(nc))
        bank = [ctx.enter_context(nc.psum_tensor(f"a_bank{i}", [P, BANK], F32)) for i in range(8)]
        hT = sb("hT", [P, KT, SEQ])
        w = sb("w_in_chunk", [P, 2, KT, SW])
        x = sb("x_tile", [P, 3, D])
        xn = sb("xn_tile", [P, 2, D])
        gain = sb("gain_attn", [P, D])
        ss = sb("sumsq_a", [P, NT])
        rstd = sb("rstd_a", [P, NT])
        ev = sb("proj_out", [P, 4, BANK])
        qk_hi, qk_lo = xn[:, :, 0:BANK], xn[:, :, BANK:D]
        hi_step, split_done = sem("qk_hi_step"), sem("qk_split")
        part_stored = [sem(f"qk_stored{i}") for i in range(2)]
        lamin = sb("lamin", [NG, 2, 2, NS])
        cin = sb("cin", [P, 2, NB, 2, NS])
        B1, B2, B1b, B2b = (sb(f"b{n}", [P, NG, GC]) for n in ("1", "2", "1bar", "2bar"))
        tb = sb("tb", [P, NG, GC])
        C1, C2 = sb("C1", [P, NG, GC]), sb("C2", [P, NG, GC])
        Dm = sb("Dm", [P, NG, GC])
        sm = sb("small", [P, 24, NG])
        smi = sb("small_int", [P, NG], I32)
        PR, PI = sb("pow_re", [P, NG, CH + 1]), sb("pow_im", [P, NG, CH + 1])
        PRr, PIr = sb("pow_re_rev", [P, NG, CH]), sb("pow_im_rev", [P, NG, CH])
        tp = sb("tp", [P, NG, CH // 2])
        anc = sb("anchor", [P, 8, 2, NG])
        TC, TS, TT = (sb(f"table_{n}", [P, GB, NCH]) for n in ("cos", "sin", "tmp"))
        Wn, Qn, Q2n = (sb(f"mat_{n}", [P, GB, CH, GC]) for n in ("w", "q", "q2"))
        junk = TT[:, 0:4, :].rearrange("p g m -> p (g m)")
        Wt = TT[:, 4:8, :].rearrange("p a (b k c) -> p (a b) k c", b=2, c=GC)
        W1, W2 = sb("mat_w1", [P, GB, P]), sb("mat_w2", [P, GB, P])
        Kt = sb("kernel_taps", [P, NG, GC])
        x_in = [sem(f"x_in{i}") for i in range(3)]
        w_in_s = [sem(f"w_in{i}") for i in range(2)]
        gain_in, param_in, bc_in = sem("gain_in"), sem("param_in"), sem("bc_in")
        sq_done, rstd_step, sqrt_done, xn_done = sem("sq_done"), sem("rstd_step"), sem("sqrt_done"), sem("xn_done")
        hT_psum, hT_done = sem("hT_psum"), sem("hT_done")
        proj_done, ev_done = sem("proj_done"), sem("ev_done")
        stored = [sem(f"proj_stored{i}") for i in range(4)]
        par_T, par_T_used, prep = sem("par_T"), sem("par_T_used"), sem("prep_step")
        sin_in, sin_out, mats, wT, wT_used = (sem(n) for n in ("sin_in", "sin_out", "mats_ready", "wT", "wT_used"))
        mats_w, d_masked = sem("mats_w"), sem("d_masked")
        mats_stored, w12_stored, taps, taps_done, taps_stored, small_in = (
            sem(n) for n in ("mats_stored", "w12_stored", "taps", "taps_done", "taps_stored", "small_in"))
        UNITS = 64
        PB = 3
        BATCH_AT = [24 + 8 * b for b in range(NB)]
        with nc.Block() as block:

            @block.sync
            def _(sp):
                for half in range(2):
                    sp.dma_start(lamin[:, 0, half, :], a["ssm_lam_re"][0]).then_inc(param_in, 16)
                    sp.dma_start(lamin[:, 1, half, :], a["ssm_lam_im"][0]).then_inc(param_in, 16)
                for v, halves in enumerate((("ssm_c_re", "ssm_c_im"), ("ssm_c_im", "ssm_c_re"))):
                    for half, name in enumerate(halves):
                        sp.dma_start(cin[:, v, :, half, :],
                                     a[name][0].rearrange("(b g) c n -> (g c) b n", g=GB)).then_inc(param_in, 16)
                sp.dma_start(gain[:], a["norm_attn"].to_broadcast([P, D])).then_inc(gain_in, 16)
                for i in range(NT):
                    if i >= 3:
                        sp.wait_ge(xn_done, i - 2)
                    sp.dma_start(x[:, i % 3, :], a["x"][0, i * P:(i + 1) * P, :]).then_inc(x_in[i % 3], 16)
                for half in range(2):
                    part = slice(half * NS, (half + 1) * NS)
                    sp.dma_start(B1[part], a["ssm_b_im" if half else "ssm_b_re"][0].rearrange("g n c -> n g c")).then_inc(bc_in, 16)
                    sp.dma_start(B2[part], a["ssm_b_re" if half else "ssm_b_im"][0].rearrange("g n c -> n g c")).then_inc(bc_in, 16)
                for n in range(UNITS):
                    c, k = chunks[n // 16], n % 16
                    if n == UNITS - 4:
                        sp.wait_ge(taps_done, 1)
                        for i in range(CH):
                            sp.dma_start(d["taps"][CH - 1 - i], Kt[i * GC:(i + 1) * GC]).then_inc(taps_stored, 16)
                    sp.wait_ge(ev_done, n + 1)
                    if c in (0, 1):
                        j = n - 16
                        sp.wait_ge(split_done, j + 1)
                        for part, t in enumerate((qk_hi, qk_lo)):
                            sp.dma_start(d["qT" if c == 0 else "kT"][part, k // 4, :, (k % 4) * BANK:(k % 4 + 1) * BANK],
                                         t[:, j % 2]).then_inc(part_stored[j % 2], 16)
                    else:
                        dst = d["u"][k // 8, k % 8] if c == 3 else d["v"][k * P:(k + 1) * P, :]
                        sp.dma_start(dst, ev[:, n % 4, :]).then_inc(stored[n % 4], 16)
                for s in range(4):
                    sp.wait_ge(stored[s], 16 * 8)
                for s in range(2):
                    sp.wait_ge(part_stored[s], 32 * 16)
                sp.wait_ge(taps_stored, 16 * CH)

            @block.gpsimd
            def _(pool):
                pool.dma_start(sm[:, 0, :], a["ssm_log_dt"].to_broadcast([P, NG])).then_inc(small_in, 16)
                pool.dma_start(Dm[:], a["ssm_d"].rearrange("l g c -> l (g c)").to_broadcast([P, NG * GC]).rearrange("p (g c) -> p g c", g=NG)).then_inc(small_in, 16)
                pool.wait_ge(small_in, 32)
                pool.affine_select(out=Dm[:], in_=Dm[:], pattern=[[0, NG], [-1, GC]], compare_op=ALU.is_equal,
                                   fill=0.0, base=-(P - GC), channel_multiplier=1).then_inc(d_masked, 1)

                def split(units):
                    for j in units:
                        pool.wait_ge(ev_done, 16 + j + 1)
                        if j >= 2:
                            pool.wait_ge(part_stored[j % 2], 32 * (j // 2))
                        pool.tensor_copy(qk_hi[:, j % 2].bitcast(F32R), ev[:, j % 4]).then_inc(hi_step, 1)
                        pool.wait_ge(hi_step, j + 1)
                        pool.tensor_tensor(qk_lo[:, j % 2].bitcast(F32R), ev[:, j % 4], qk_hi[:, j % 2], ALU.subtract).then_inc(split_done, 1)

                for n, c in enumerate(chunks):
                    if n >= 2:
                        pool.wait_ge(proj_done, 16 * (n - 1))
                    pool.dma_start(w[:, n % 2], a["w_in"][0].rearrange("(p k) n -> p k n", k=KT)[:, :, c * SW:(c + 1) * SW]
                                   ).then_inc(w_in_s[n % 2], 16)
                    if n == 2:
                        split(range(0, 16))
                split(range(16, 32))

            @block.scalar
            def _(act):
                act.wait_ge(par_T, 1)
                step = Step(act, par_T_used)
                step(act.activation(sm[:, 1:3, :], bank[0][:, 0:2 * NG].rearrange("p (a g) -> p a g", a=2), ACT.Copy))
                c1v, c2v = (bank[i][:].rearrange("p (g c) -> p g c", g=NG) for i in (1, 2))
                step(act.activation(C1[0:NS], c1v[0:NS], ACT.Copy))
                step(act.activation(C1[NS:P], c1v[NS:P], ACT.Copy, scale=-1.0))
                step(act.activation(C2[:], c2v, ACT.Copy, scale=-1.0))
                for i in range(NT):
                    act.wait_ge(x_in[i % 3], 16 * (i // 3 + 1))
                    if i:
                        act.wait_ge(sq_done, i)
                    act.activation(junk, x[:, i % 3, :], ACT.Square, accum_out=ss[:, i:i + 1]).then_inc(sq_done, 1)
                    act.wait_ge(rstd_step, 2 * i + 1)
                    act.activation(rstd[:, i:i + 1], rstd[:, i:i + 1], ACT.Sqrt).then_inc(sqrt_done, 1)
                    for h in range(2):
                        n = 2 * i - 2 + h
                        if n >= 0:
                            act.wait_ge(hT_psum, n + 1)
                            act.activation(hT[:, 4 * h:4 * h + 4, (i - 1) * P:i * P],
                                           bank[n % 4][:].rearrange("p (k t) -> p k t", k=4), ACT.Copy).then_inc(hT_done, 1)
                for h in range(2):
                    n = 2 * NT - 2 + h
                    act.wait_ge(hT_psum, n + 1)
                    act.activation(hT[:, 4 * h:4 * h + 4, (NT - 1) * P:NT * P],
                                   bank[n % 4][:].rearrange("p (k t) -> p k t", k=4), ACT.Copy).then_inc(hT_done, 1)

                def sines():
                    act.wait_ge(sin_in, 1)
                    act.activation(sm[:, 7:9, :], sm[:, 7:9, :], ACT.Sin).then_inc(sin_out, 1)

                def batch(b):
                    for q in range(2):
                        act.wait_ge(wT, 2 * b + q + 1)
                        if b and q == 0:
                            act.wait_ge(w12_stored, 32 * b)
                        v = bank[2 * (b % 2) + q][:].rearrange("p (g n) -> p g n", g=4)
                        gs = slice(4 * q, 4 * q + 4)
                        act.activation(W1[:, gs, :], v, ACT.Copy).then_inc(wT_used, 1)
                        act.activation(W2[:, gs, 0:NS], v[:, :, NS:P], ACT.Copy).then_inc(wT_used, 1)
                        act.activation(W2[:, gs, NS:P], v[:, :, 0:NS], ACT.Copy, scale=-1.0).then_inc(wT_used, 1)
                    act.wait_ge(wT_used, 6 * (b + 1))
                    act.dma_start(d["w1"][b], W1[:]).then_inc(w12_stored, 16)
                    act.dma_start(d["w2"][b], W2[:]).then_inc(w12_stored, 16)
                    act.wait_ge(mats, 2 * (b + 1))
                    for name, t in (("q", Qn), ("q2", Q2n), ("cos", TC), ("sin", TS)):
                        act.dma_start(d[name][b], t[:]).then_inc(mats_stored, 16)

                sines()
                for n in range(UNITS):
                    if n in BATCH_AT:
                        batch(BATCH_AT.index(n))
                    act.wait_ge(proj_done, n + 1)
                    if 20 <= n < 52:
                        act.wait_ge(split_done, n - 19)
                    elif n >= 4:
                        act.wait_ge(stored[n % 4], 16 * (n // 4 if n < 20 else n // 4 - 8))
                    act.activation(ev[:, n % 4, :], bank[4 + n % PB][:], ACT.Copy,
                                   scale=HD ** -0.5 if chunks[n // 16] == 0 else 1.0).then_inc(ev_done, 1)
                act.wait_ge(w12_stored, 32 * NB)
                act.wait_ge(mats_stored, 64 * NB)

            @block.vector
            def _(dve):
                for i in range(NT):
                    dve.wait_ge(sq_done, i + 1)
                    dve.tensor_scalar(rstd[:, i:i + 1], ss[:, i:i + 1], 1.0 / D, EPS, ALU.mult, ALU.add).then_inc(rstd_step, 1)
                    dve.wait_ge(sqrt_done, i + 1)
                    dve.reciprocal(rstd[:, i:i + 1], rstd[:, i:i + 1]).then_inc(rstd_step, 1)
                    dve.wait_ge(rstd_step, 2 * i + 2)
                    if i == 0:
                        dve.wait_ge(gain_in, 16)
                    if i >= 2:
                        dve.wait_ge(hT_psum, 2 * (i - 1))
                    dve.scalar_tensor_tensor(xn[:, i % 2, :], x[:, i % 3, :], rstd[:, i:i + 1], gain[:],
                                             ALU.mult, ALU.mult).then_inc(xn_done, 1)
                step = Step(dve, prep)
                s = lambda k: sm[:, k, :]
                dve.wait_ge(small_in, 32)
                dve.wait_ge(par_T_used, 4)
                dve.wait_ge(d_masked, 1)
                exact_exp(step, dve, s(3), s(0), s(4), s(5), smi[:])
                step(dve.tensor_tensor(s(4), s(1), s(3), ALU.mult))
                step(dve.tensor_tensor(s(7), s(2), s(3), ALU.mult))
                exact_exp(step, dve, s(5), s(4), s(6), s(9), smi[:])
                step(dve.tensor_scalar(s(6), s(7), 1.0 / (2 * math.pi), 12582912.0, ALU.mult, ALU.add))
                step(dve.tensor_scalar(s(6), s(6), -12582912.0, None, ALU.add))
                two_pi = [6.28125, 0.0019350051879882812, 3.01991623e-07]
                for c in two_pi:
                    step(dve.scalar_tensor_tensor(s(7), s(6), -c, s(7), ALU.mult, ALU.add))
                step(dve.tensor_scalar(s(7), s(7), 3.1415925, -3.1415925, ALU.min, ALU.max))
                step(dve.tensor_scalar(s(8), s(7), -1.0, None, ALU.mult))
                step(dve.tensor_tensor(s(8), s(7), s(8), ALU.max))
                dve.tensor_scalar(s(8), s(8), -1.0, math.pi / 2, ALU.mult, ALU.add).then_inc(sin_in, 1)
                dve.wait_ge(sin_out, 1)
                step(dve.tensor_tensor(PR[:, :, 1], s(5), s(8), ALU.mult))
                step(dve.tensor_tensor(PI[:, :, 1], s(5), s(7), ALU.mult))
                step(dve.memset(PR[:, :, 0], 1.0))
                step(dve.memset(PI[:, :, 0], 0.0))
                step(dve.tensor_tensor(s(10), s(1), s(1), ALU.mult))
                step(dve.tensor_tensor(s(11), s(2), s(2), ALU.mult))
                step(dve.tensor_tensor(s(10), s(10), s(11), ALU.add))
                step(dve.reciprocal(s(10), s(10)))
                step(dve.tensor_scalar(s(11), PR[:, :, 1], -1.0, None, ALU.add))
                step(dve.tensor_tensor(s(12), s(11), s(1), ALU.mult))
                step(dve.tensor_tensor(s(13), PI[:, :, 1], s(2), ALU.mult))
                step(dve.tensor_tensor(s(12), s(12), s(13), ALU.add))
                step(dve.tensor_tensor(s(12), s(12), s(10), ALU.mult))
                step(dve.tensor_tensor(s(13), PI[:, :, 1], s(1), ALU.mult))
                step(dve.tensor_tensor(s(14), s(11), s(2), ALU.mult))
                step(dve.tensor_tensor(s(13), s(13), s(14), ALU.subtract))
                step(dve.tensor_tensor(s(13), s(13), s(10), ALU.mult))
                dve.wait_ge(bc_in, 64)
                step(dve.tensor_scalar(B2[0:NS], B2[0:NS], -1.0, None, ALU.mult))
                fr = s(12).rearrange("p (g o) -> p g o", o=1).to_broadcast([P, NG, GC])
                fi = s(13).rearrange("p (g o) -> p g o", o=1).to_broadcast([P, NG, GC])
                step(dve.tensor_tensor(B1b[:], B1[:], fr, ALU.mult))
                step(dve.tensor_tensor(tb[:], B2[:], fi, ALU.mult))
                step(dve.tensor_tensor(B1b[:], B1b[:], tb[:], ALU.add))
                step(dve.tensor_tensor(B2b[:], B2[:], fr, ALU.mult))
                step(dve.tensor_tensor(tb[:], B1[:], fi, ALU.mult))
                step(dve.tensor_tensor(B2b[:], B2b[:], tb[:], ALU.subtract))
                k = 1
                while k < CH:
                    br, bi = (t[:, :, k:k + 1].to_broadcast([P, NG, k]) for t in (PR, PI))
                    complex_mul(step, dve, PR[:, :, k + 1:2 * k + 1], PI[:, :, k + 1:2 * k + 1],
                                PR[:, :, 1:k + 1], PI[:, :, 1:k + 1], br, bi, tp[:, :, 0:k])
                    k *= 2
                for i in range(CH):
                    step(dve.tensor_copy(PRr[:, :, i], PR[:, :, CH - 1 - i]))
                    step(dve.tensor_copy(PIr[:, :, i], PI[:, :, CH - 1 - i]))
                step(dve.tensor_tensor(s(15), s(5), s(5), ALU.mult))
                step(dve.tensor_tensor(s(15), s(15), s(15), ALU.mult))
                step(dve.tensor_tensor(r8[:], s(15), s(15), ALU.mult))
                cur = (s(8), s(7))
                for k in range(11):
                    if k < 3:
                        nxt = (s(16 + 2 * (k % 2)), s(17 + 2 * (k % 2)))
                        if k == 2:
                            nxt = (anc[:, 0, 0, :], anc[:, 0, 1, :])
                    elif k < 10:
                        nxt = (anc[:, k - 2, 0, :], anc[:, k - 2, 1, :])
                    else:
                        break
                    complex_mul(step, dve, nxt[0], nxt[1], cur[0], cur[1], cur[0], cur[1], s(20))
                    step(dve.tensor_tensor(s(20), nxt[0], nxt[0], ALU.mult))
                    step(dve.tensor_tensor(s(21), nxt[1], nxt[1], ALU.mult))
                    step(dve.tensor_tensor(s(20), s(20), s(21), ALU.add))
                    step(dve.tensor_scalar(s(20), s(20), -0.5, 1.5, ALU.mult, ALU.add))
                    step(dve.tensor_tensor(nxt[0], nxt[0], s(20), ALU.mult))
                    step(dve.tensor_tensor(nxt[1], nxt[1], s(20), ALU.mult))
                    cur = nxt
                for b in range(NB):
                    gs = slice(b * GB, (b + 1) * GB)
                    up = lambda t: t.rearrange("p g (k o) -> p g k o", o=1).to_broadcast([P, GB, CH, GC])
                    across = lambda t: t.rearrange("p g (o c) -> p g o c", o=1).to_broadcast([P, GB, CH, GC])
                    if b:
                        dve.wait_ge(mats_stored, 64 * b)
                        dve.wait_ge(taps, b)
                    step(dve.tensor_tensor(Wn[:], up(PRr[:, gs]), across(B1b[:, gs]), ALU.mult))
                    step(dve.tensor_tensor(Wt, up(PIr[:, gs]), across(B2b[:, gs]), ALU.mult))
                    dve.tensor_tensor(Wn[:], Wn[:], Wt, ALU.add).then_inc(mats_w, 1)
                    dve.wait_ge(mats_w, b + 1)
                    step(dve.tensor_tensor(Qn[:], up(PR[:, gs, 1:]), across(C1[:, gs]), ALU.mult))
                    step(dve.tensor_tensor(Wt, up(PI[:, gs, 1:]), across(C2[:, gs]), ALU.mult))
                    step(dve.tensor_tensor(Qn[:], Qn[:], Wt, ALU.add))
                    step(dve.tensor_tensor(Q2n[:], up(PR[:, gs, 1:]), across(C2[:, gs]), ALU.mult))
                    step(dve.tensor_tensor(Wt, up(PI[:, gs, 1:]), across(C1[:, gs]), ALU.mult))
                    dve.tensor_tensor(Q2n[:], Q2n[:], Wt, ALU.subtract).then_inc(mats, 1)
                    step(dve.memset(TC[:, :, 0:1], 1.0))
                    step(dve.memset(TS[:, :, 0:1], 0.0))
                    k = 1
                    for e in range(8):
                        br, bi = (anc[:, e, r, gs].rearrange("p (g o) -> p g o", o=1).to_broadcast([P, GB, k]) for r in (0, 1))
                        complex_mul(step, dve, TC[:, :, k:2 * k], TS[:, :, k:2 * k], TC[:, :, 0:k], TS[:, :, 0:k],
                                    br, bi, TT[:, :, 0:k])
                        k *= 2
                    dve.tensor_copy(TT[:, :, 0:1], TC[:, :, 0:1]).then_inc(mats, 1)
                dve.wait_ge(taps, NB)
                dve.tensor_tensor(Kt[:], bank[7][:].rearrange("p (g c) -> p g c", g=NG), Dm[:],
                                  ALU.add).then_inc(taps_done, 1)

            @block.tensor
            def _(pe):
                pe.wait_ge(param_in, 16 * 8)
                for r in range(2):
                    pe.transpose(bank[0][:, r * NG:(r + 1) * NG], lamin[:, r].rearrange("g h n -> g (h n)"),
                                 ident[0:NG, 0:NG])
                for v in range(2):
                    for b in range(NB):
                        last = pe.transpose(bank[1 + v][:, b * P:(b + 1) * P], cin[:, v, b].rearrange("p h n -> p (h n)"), ident[:])
                last.then_inc(par_T, 1)
                pe.wait_ge(par_T_used, 4)
                for i in range(NT):
                    pe.wait_ge(xn_done, i + 1)
                    for h in range(2):
                        n = 2 * i + h
                        if n >= 4:
                            pe.wait_ge(hT_done, n - 3)
                        for k in range(4):
                            last = pe.transpose(bank[n % 4][:, k * P:(k + 1) * P], xn[:, i % 2, 4 * h + k:D:KT], ident[:])
                        last.then_inc(hT_psum, 1)
                pe.wait_ge(hT_done, 2 * NT)

                def batch(b):
                    pe.wait_ge(mats_w, b + 1)
                    for q in range(2):
                        if b >= 2:
                            pe.wait_ge(wT_used, 6 * (b - 1))
                        for g in range(4):
                            last = pe.transpose(bank[2 * (b % 2) + q][:, g * P:(g + 1) * P],
                                                Wn[:, 4 * q + g].rearrange("p i c -> p (i c)"), ident[:])
                        last.then_inc(wT, 1)

                def tap(b):
                    for g in range(GB):
                        last = pe.matmul(bank[7][:, (b * GB + g) * GC:(b * GB + g + 1) * GC],
                                         Wn[:, g].rearrange("p i c -> p (i c)"), C1[:, b * GB + g], start=True, stop=True)
                    last.then_inc(taps, 1)

                for n in range(UNITS):
                    c, k = chunks[n // 16], n % 16
                    if n in BATCH_AT:
                        batch(BATCH_AT.index(n))
                        tap(BATCH_AT.index(n))
                    if k == 0:
                        pe.wait_ge(w_in_s[(n // 16) % 2], 16 * (n // 32 + 1))
                    if n >= PB:
                        pe.wait_ge(ev_done, n - PB + 1)
                    wc = w[:, (n // 16) % 2]
                    for kt in range(KT):
                        if c == 3:
                            lhsT, rhs = hT[:, kt, (k // 8) * 1024 + k % 8:(k // 8 + 1) * 1024:CH], wc[:, kt, :]
                        elif c == 2:
                            lhsT, rhs = hT[:, kt, k * P:(k + 1) * P], wc[:, kt, :]
                        else:
                            lhsT, rhs = wc[:, kt, (k // 4) * P:(k // 4 + 1) * P], hT[:, kt, (k % 4) * BANK:(k % 4 + 1) * BANK]
                        last = pe.matmul(bank[4 + n % PB][:], lhsT, rhs, start=kt == 0, stop=kt == KT - 1)
                    last.then_inc(proj_done, 1)


def s5_groups(nc, ident, r8, U, a, d):
    NP = NG // 2
    with ExitStack() as ctx:
        sb = lambda name, shape, dt=F32: ctx.enter_context(nc.sbuf_tensor(name, shape, dt))
        sem = ctx.enter_context(phase_semaphores(nc))
        bank = [ctx.enter_context(nc.psum_tensor(f"b_bank{i}", [P, BANK], F32)) for i in range(8)]
        Ut = sb("u_by_group", [P, 2, NG, CH, GC])
        M = sb("taps_toeplitz", [P, CH, SW])
        Wb = sb("w_batch", [P, 2, 2, GB, P])
        Qb = sb("q_batch", [P, 2, 2, GB, CH * GC])
        Tb = sb("table_batch", [P, 2, 2, GB, NCH])
        Ug = sb("u_group", [P, 3, 2, NCH])
        zi = sb("z_in", [P, 2, 2, NCH])
        zt = sb("z_tmp", [P, 2, NCH])
        z = sb("z_state", [P, 2, 2, NCH])
        cz, sz = sb("cos_z", [P, 2, 2, NCH]), sb("sin_z", [P, 2, 2, NCH])
        u_in = [sem(f"u_in{i}") for i in range(2)]
        m_zero, m_in, regrouped = sem("m_zero"), sem("m_in"), sem("regrouped")
        batch_in = [sem(f"batch_in{i}") for i in range(2)]
        uT, ug_ready, v_done = sem("uT"), sem("ug_ready"), sem("v_done")
        v_used, z_in_done, z_done, cz_zero, cz_done, sz_done = (
            sem(n) for n in ("v_used", "z_in_done", "z_done", "cz_zero", "cz_done", "sz_done"))
        y_done, y_used = sem("y_done"), sem("y_used")
        with nc.Block() as block:

            @block.sync
            def _(sp):
                for h in range(2):
                    sp.dma_start(U[:, h], d["u"][h].rearrange("j m c -> m j c")).then_inc(u_in[h], 16)
                for b in range(NB):
                    if b >= 2:
                        sp.wait_ge(y_done, 4 * (b - 1))
                    for r, name in enumerate(("w1", "w2")):
                        sp.dma_start(Wb[:, b % 2, r], d[name][b]).then_inc(batch_in[b % 2], 16)
                    for r, name in enumerate(("cos", "sin")):
                        sp.dma_start(Tb[:, b % 2, r], d[name][b]).then_inc(batch_in[b % 2], 16)
                    for r, name in enumerate(("q", "q2")):
                        sp.dma_start(Qb[:, b % 2, r], d[name][b].rearrange("p g k c -> p g (k c)")).then_inc(batch_in[b % 2], 16)
                    if b == 0:
                        sp.wait_ge(m_zero, 1)
                        for i in range(CH):
                            sp.dma_start(M[i * GC:(i + 1) * GC, i:, :], d["taps"][0:CH - i].rearrange("t q g c -> q t (g c)")
                                         ).then_inc(m_in, 16)

            @block.gpsimd
            def _(pool):
                pool.memset(cz[:, :, :, 0:1], 0.0).then_inc(cz_zero, 1)
                pool.memset(sz[:, :, :, 0:1], 0.0).then_inc(cz_zero, 1)
                for p in range(NP):
                    b, g = p // 4, 2 * (p % 4)
                    pool.wait_ge(z_done, 2 * (p + 1))
                    if p >= 2:
                        pool.wait_ge(y_done, p - 1)
                    pool.tensor_tensor(cz[:, p % 2, :, 1:], z[:, p % 2, :, 0:NCH - 1], Tb[:, b % 2, 0, g:g + 2, 0:NCH - 1],
                                       ALU.mult).then_inc(cz_done, 1)
                    pool.tensor_tensor(sz[:, p % 2, :, 1:], z[:, p % 2, :, 0:NCH - 1], Tb[:, b % 2, 1, g:g + 2, 0:NCH - 1],
                                       ALU.mult).then_inc(sz_done, 1)

            @block.vector
            def _(dve):
                dve.memset(M[:], 0.0).then_inc(m_zero, 1)
                for h in range(2):
                    dve.wait_ge(u_in[h], 16)
                    for j in range(CH):
                        dve.tensor_copy(Ut[:, h, :, j], U[:, h, j].rearrange("m (g c) -> m g c", c=GC)).then_inc(regrouped, 1)
                for p in range(NP):
                    b, g = p // 4, 2 * (p % 4)
                    v1, v2 = (bank[2 + 2 * (p % 2) + r][:].rearrange("p (g m) -> p g m", g=2) for r in range(2))
                    dve.wait_ge(v_done, p + 1)
                    if p >= 2:
                        dve.wait_ge(z_done, 2 * (p - 1))
                    if p:
                        dve.wait_ge(z_in_done, p)
                    dve.tensor_tensor(zi[:, p % 2], v1, Tb[:, b % 2, 0, g:g + 2], ALU.mult).then_inc(v_used, 1)
                    dve.tensor_tensor(zt[:], v2, Tb[:, b % 2, 1, g:g + 2], ALU.mult).then_inc(v_used, 1)
                    dve.wait_ge(v_used, 2 * (p + 1))
                    dve.tensor_tensor(zi[:, p % 2], zi[:, p % 2], zt[:], ALU.add).then_inc(z_in_done, 1)
                    dve.wait_ge(z_in_done, p + 1)
                    if p >= 2:
                        dve.wait_ge(sz_done, p - 1)
                        dve.wait_ge(cz_done, p - 1)
                    for e in range(2):
                        G = 2 * p + e
                        dve.tensor_tensor_scan(z[:, p % 2, e], r8[:, G:G + 1].to_broadcast([P, NCH]), zi[:, p % 2, e], 0.0,
                                               ALU.mult, ALU.add).then_inc(z_done, 1)

            @block.scalar
            def _(act):
                def gelu(p):
                    act.wait_ge(y_done, p + 1)
                    if p == 0:
                        act.wait_ge(regrouped, 2 * CH)
                    for e in range(2):
                        G = 2 * p + e
                        y = bank[6 + p % 2][:, e * NCH:(e + 1) * NCH].rearrange("m (h j c) -> m h j c", h=2, c=GC)
                        act.activation(U[:, :, :, G * GC:(G + 1) * GC], y, ACT.Gelu_apprx_tanh).then_inc(y_used, 1)
                for p in range(NP):
                    act.wait_ge(uT, p + 1)
                    if p >= 3:
                        act.wait_ge(y_done, p - 2)
                    act.activation(Ug[:, p % 3], bank[p % 2][:].rearrange("p (g m) -> p g m", g=2), ACT.Copy).then_inc(ug_ready, 1)
                    if p >= 2:
                        gelu(p - 2)
                gelu(NP - 2)
                gelu(NP - 1)

            @block.tensor
            def _(pe):
                def u_T(p):
                    if p >= 2:
                        pe.wait_ge(ug_ready, p - 1)
                    if p == 0:
                        pe.wait_ge(regrouped, 2 * CH)
                    for e in range(2):
                        for h in range(2):
                            G = 2 * p + e
                            last = pe.transpose(bank[p % 2][:, e * NCH + h * P:e * NCH + (h + 1) * P],
                                                Ut[:, h, G].rearrange("m j c -> m (j c)"), ident[:])
                    last.then_inc(uT, 1)

                def states(p):
                    b, g = p // 4, 2 * (p % 4)
                    if p % 4 == 0:
                        pe.wait_ge(batch_in[b % 2], 16 * 6 * (b // 2 + 1))
                    pe.wait_ge(ug_ready, p + 1)
                    if p >= 2:
                        pe.wait_ge(v_used, 2 * (p - 1))
                    for r in range(2):
                        for e in range(2):
                            last = pe.matmul(bank[2 + 2 * (p % 2) + r][:, e * NCH:(e + 1) * NCH], Wb[:, b % 2, r, g + e],
                                             Ug[:, p % 3, e], start=True, stop=True)
                    last.then_inc(v_done, 1)

                def outputs(p):
                    b, g = p // 4, 2 * (p % 4)
                    if p == 0:
                        pe.wait_ge(m_in, 16 * CH)
                        pe.wait_ge(cz_zero, 2)
                    if p >= 2:
                        pe.wait_ge(y_used, 2 * (p - 1))
                    pe.wait_ge(cz_done, p + 1)
                    pe.wait_ge(sz_done, p + 1)
                    for e in range(2):
                        G = 2 * p + e
                        for h in range(2):
                            o = bank[6 + p % 2][:, e * NCH + h * P:e * NCH + (h + 1) * P]
                            ms = slice(h * P, (h + 1) * P)
                            pe.matmul(o, Ug[:, p % 3, e, ms], M[:, :, G * GC:(G + 1) * GC], start=True, stop=False)
                            pe.matmul(o, cz[:, p % 2, e, ms], Qb[:, b % 2, 0, g + e], start=False, stop=False)
                            last = pe.matmul(o, sz[:, p % 2, e, ms], Qb[:, b % 2, 1, g + e], start=False, stop=True)
                    last.then_inc(y_done, 1)

                for p in range(2):
                    u_T(p)
                    states(p)
                for p in range(NP):
                    if p + 2 < NP:
                        u_T(p + 2)
                    outputs(p)
                    if p + 2 < NP:
                        states(p + 2)


def s5_gate(nc, ident, ones, Y, srs, a, d):
    with ExitStack() as ctx:
        sb = lambda name, shape, dt=F32: ctx.enter_context(nc.sbuf_tensor(name, shape, dt))
        sem = ctx.enter_context(phase_semaphores(nc))
        bank = [ctx.enter_context(nc.psum_tensor(f"g_bank{i}", [P, BANK], F32)) for i in range(8)]
        yT = sb("yT", [P, 4, SEQ])
        wg = sb("w_glu", [P, 4, SW])
        bg, gg = sb("b_glu", [P, 4]), sb("ssm_gain", [P, 4])
        sg = sb("sigmoid", [P, 2, BANK])
        z = sb("gated", [P, 2, BANK])
        sq = sb("squares", [P, 2, 4, BANK])
        ssmT = sb("ssmT", [P, 4, SEQ])
        ssm_st = sem("ssmT_stored")
        zero = sb("zero_rows", [P, D])
        zero_set, zero_st = sem("zero_set"), sem("zero_rows_stored")
        ld, yT_psum, yT_done, glu_done, sig_done = (sem(n) for n in ("glu_in", "yT_psum", "yT_done", "glu_done", "sig_done"))
        gated, squared, scaled, sum_done, fin = (sem(n) for n in ("gated", "squared", "scaled", "sum_done", "ssm_rms"))
        with nc.Block() as block:

            @block.gpsimd
            def _(pool):
                pool.memset(zero[:], 0.0).then_inc(zero_set, 1)
                pool.wait_ge(zero_set, 1)
                for b in range(MIN_BLK, NBLK + 2):
                    pool.dma_start(d["rows"][b], zero[:]).then_inc(zero_st, 16)
                pool.wait_ge(zero_st, 16 * (NBLK + 2 - MIN_BLK))

            @block.sync
            def _(sp):
                sp.dma_start(wg[:], a["w_glu"][0].rearrange("(k p) n -> p k n", p=P)).then_inc(ld, 16)
                sp.dma_start(bg[:], a["b_glu"][0].rearrange("(k p) -> p k", p=P), allow_slow_non_contiguous=True).then_inc(ld, 16)
                sp.dma_start(gg[:], a["ssm_norm"][0].rearrange("(k p) -> p k", p=P), allow_slow_non_contiguous=True).then_inc(ld, 16)
                for t in range(4):
                    sp.wait_ge(scaled, 4 * (t + 1))
                    cols = slice(t * BANK, (t + 1) * BANK)
                    sp.dma_start(d["ssmT"][:, :, cols], ssmT[:, :, cols]).then_inc(ssm_st, 16)
                sp.wait_ge(ssm_st, 64)

            @block.scalar
            def _(act):
                yTv = yT[:].rearrange("p k (h m j) -> p k h m j", h=2, j=CH)
                for n in range(2 * CH):
                    act.wait_ge(yT_psum, n + 1)
                    act.activation(yTv[:, :, n // CH, :, n % CH], bank[n % 4][:].rearrange("p (k m) -> p k m", k=4),
                                   ACT.Copy).then_inc(yT_done, 1)
                act.wait_ge(ld, 48)
                for n in range(16):
                    act.wait_ge(glu_done, n + 1)
                    if n >= 2:
                        act.wait_ge(gated, n - 1)
                    act.activation(sg[:, n % 2], bank[4 + n % 3][:], ACT.Sigmoid, bias=bg[:, n % 4:n % 4 + 1]).then_inc(sig_done, 1)
                act.wait_ge(fin, 1)
                act.activation(srs[:], srs[:], ACT.Sqrt).then_inc(fin, 1)

            @block.vector
            def _(dve):
                for n in range(16):
                    t, oc = n // 4, n % 4
                    cols = slice(t * BANK, (t + 1) * BANK)
                    dve.wait_ge(sig_done, n + 1)
                    if n >= 2:
                        dve.wait_ge(scaled, n - 1)
                        dve.wait_ge(squared, n - 1)
                    dve.tensor_tensor(z[:, n % 2], yT[:, oc, cols], sg[:, n % 2], ALU.mult).then_inc(gated, 1)
                    dve.wait_ge(gated, n + 1)
                    if t >= 2:
                        dve.wait_ge(sum_done, t - 1)
                    dve.tensor_tensor(sq[:, t % 2, oc], z[:, n % 2], z[:, n % 2], ALU.mult).then_inc(squared, 1)
                    dve.tensor_scalar(ssmT[:, oc, cols], z[:, n % 2], gg[:, oc:oc + 1], None, ALU.mult).then_inc(scaled, 1)
                dve.wait_ge(sum_done, 4)
                dve.tensor_scalar(srs[:], bank[7][:, 0:NT], 1.0 / SW, EPS, ALU.mult, ALU.add).then_inc(fin, 1)
                dve.wait_ge(fin, 2)
                dve.reciprocal(srs[:], srs[:]).then_inc(fin, 1)
                dve.wait_ge(fin, 3)

            @block.tensor
            def _(pe):
                for n in range(2 * CH):
                    if n >= 4:
                        pe.wait_ge(yT_done, n - 3)
                    for k in range(4):
                        last = pe.transpose(bank[n % 4][:, k * P:(k + 1) * P], Y[:, n // CH, n % CH, k * P:(k + 1) * P], ident[:])
                    last.then_inc(yT_psum, 1)
                pe.wait_ge(yT_done, 2 * CH)
                pe.wait_ge(ld, 48)

                def sums(t):
                    pe.wait_ge(squared, 4 * (t + 1))
                    for i in range(4):
                        for k in range(4):
                            last = pe.matmul(bank[7][:, 4 * t + i:4 * t + i + 1], sq[:, t % 2, k, i * P:(i + 1) * P], ones[:, 0:1],
                                             start=k == 0, stop=k == 3)
                    last.then_inc(sum_done, 1)

                for n in range(16):
                    t, oc = n // 4, n % 4
                    if n >= 3:
                        pe.wait_ge(sig_done, n - 2)
                    for k in range(4):
                        last = pe.matmul(bank[4 + n % 3][:], wg[:, k, oc * P:(oc + 1) * P], yT[:, k, t * BANK:(t + 1) * BANK],
                                         start=k == 0, stop=k == 3)
                    last.then_inc(glu_done, 1)
                    if n % 4 == 1 and t:
                        sums(t - 1)
                sums(3)


def attention(nc, ident, oT, wo, a, d):
    UN = HEADS * NT
    SLOTS = 3
    slopes = [2.0 ** (-8.0 * (h + 1) / HEADS) for h in range(HEADS)]
    GRP = 4
    width = lambda u: (u % NT + 1) * P
    chunks_of = lambda u: (u % NT + 1 + GRP - 1) // GRP
    qk_before = [0]
    tr_before = [0]
    for u in range(UN):
        qk_before.append(qk_before[-1] + 2 * chunks_of(u))
        tr_before.append(tr_before[-1] + chunks_of(u))
    FIN_AT = [(h + 1) * NT + 4 for h in range(HEADS - 1)]
    with ExitStack() as ctx:
        sb = lambda name, shape, dt=F32: ctx.enter_context(nc.sbuf_tensor(name, shape, dt))
        sem = ctx.enter_context(phase_semaphores(nc))
        bank = [ctx.enter_context(nc.psum_tensor(f"c_bank{i}", [P, BANK], F32)) for i in range(8)]
        q, kh, kl = (sb(n, [P, 2, SEQ]) for n in ("q_parts", "k_hi", "k_lo"))
        v = sb("v_head", [P, 2, NT, VD])
        bias = sb("alibi", [P, 2, SEQ])
        S = sb("scores", [P, SLOTS, 2, SEQ])
        mx, nm, rs = sb("max_part", [P, SLOTS, 2, 4]), sb("neg_max", [P, SLOTS, 2]), sb("row_sum", [P, SLOTS, 2])
        ri, c2 = sb("row_inv", [P, SLOTS, 2]), sb("map2_scale", [P, SLOTS, 1])
        aT = sb("map_T", [P, 2, BANK])
        o = sb("o_head", [P, 2, NT, VD])
        sqj, oss = sb("o_sq", [P, VD]), sb("o_sumsq", [P, 2, NT])
        lv, lj = sb("lam_vecs", [P, 4, HD]), sb("lam_prod", [P, HD])
        ls = sb("lam_small", [P, 6, 2])
        lsi = sb("lam_int", [P, 2], I32)
        gain = sb("subln", [P, 1])
        qk_in = [sem(f"qk_in{c}") for c in range(4)]
        v_in = [sem(f"v_in{i}") for i in range(2)]
        wo_in = sem("w_out_in")
        lam_in, lam_step, bias_step, bias_ready, gain_ready = (sem(n) for n in ("lam_in", "lam_step", "bias_step", "bias_ready", "gain_ready"))
        qk_done, scored, maxed, exped, inv_step, mixed = (
            sem(n) for n in ("qk_done", "scored", "maxed", "exped", "inv_step", "mixed"))
        mapT, aT_ready, pv_chunk, o_used, o_sq = (sem(n) for n in ("mapT", "aT_ready", "pv_chunk", "o_used", "o_sq"))
        fin_dve, fin_act, fin_T, fin_out = (sem(n) for n in ("fin_dve", "fin_act", "fin_T", "fin_out"))
        with nc.Block() as block:

            @block.sync
            def _(sp):
                for n, name in enumerate(("lambda_q1", "lambda_k1", "lambda_q2", "lambda_k2")):
                    sp.dma_start(lv[:, n], a[name].to_broadcast([P, HD])).then_inc(lam_in, 16)
                sp.dma_start(gain[:], a["attn_subln"].rearrange("l (v o) -> (l v) o", o=1)).then_inc(lam_in, 16)
                def load_v(h):
                    if h >= 2:
                        sp.wait_ge(pv_chunk, tr_before[NT * (h - 1)])
                    sp.dma_start(v[:, h % 2], d["v"].rearrange("(t p) c -> p t c", p=P)[:, :, h * VD:(h + 1) * VD]
                                 ).then_inc(v_in[h % 2], 16)

                for h in range(HEADS):
                    if h:
                        sp.wait_ge(qk_done, qk_before[NT * h])
                    top, low = slice(0, HD), slice(HD, P)
                    for c in range(4):
                        cols = slice(c * BANK, (c + 1) * BANK)
                        src = lambda name, part: d[name][part, h].rearrange("(m p) t -> p m t", m=2)[:, :, cols]
                        for tile, rows, name, part in ((q, top, "qT", 0), (q, low, "qT", 1), (kh, top, "kT", 0),
                                                       (kh, low, "kT", 0), (kl, top, "kT", 1), (kl, low, "kT", 1)):
                            sp.dma_start(tile[rows, :, cols], src(name, part)).then_inc(qk_in[c], 16)
                        if c == 0:
                            load_v(h)
                    if h == 0:
                        sp.dma_start(wo[:], a["w_out"][0].rearrange("(k p) n -> p k n", p=P)[:, :, 0:BANK]).then_inc(wo_in, 16)
                sp.wait_ge(wo_in, 16)

            @block.gpsimd
            def _(pool):
                def make_bias(h):
                    if h >= 2:
                        pool.wait_ge(scored, qk_before[NT * (h - 1)])
                    t, ti = bias[:, h % 2], bias[:, h % 2].bitcast(I32)
                    pool.iota(ti, pattern=[[1, SEQ]], base=-(SEQ - P), channel_multiplier=-1).then_inc(bias_step, 1)
                    if h:
                        pool.wait_ge(bias_step, 3 * h + 1)
                        pool.tensor_copy(t, ti).then_inc(bias_step, 1)
                        pool.wait_ge(bias_step, 3 * h + 2)
                        pool.tensor_scalar(t, t, slopes[h], None, ALU.mult).then_inc(bias_step, 1)
                    pool.wait_ge(bias_step, 3 * h + 3)
                    pool.affine_select(out=t, in_=t, pattern=[[-1, SEQ]], compare_op=ALU.is_ge,
                                       fill=-BIG, base=SEQ - P, channel_multiplier=1).then_inc(bias_ready, 1)

                make_bias(0)
                make_bias(1)
                make_bias(2)
                make_bias(3)

            @block.vector
            def _(dve):
                dve.wait_ge(bias_step, 1)
                dve.tensor_copy(bias[:, 0], bias[:, 0].bitcast(I32)).then_inc(bias_step, 1)
                dve.wait_ge(bias_step, 2)
                dve.tensor_scalar(bias[:, 0], bias[:, 0], slopes[0], None, ALU.mult).then_inc(bias_step, 1)
                dve.wait_ge(lam_in, 80)
                step = Step(dve, lam_step)
                for m in range(2):
                    step(dve.tensor_tensor(lj[:], lv[:, 2 * m], lv[:, 2 * m + 1], ALU.mult))
                    step(dve.tensor_reduce(ls[:, 0, m:m + 1], lj[:], AX.X, ALU.add))
                exact_exp(step, dve, ls[:, 1], ls[:, 0], ls[:, 2], ls[:, 3], lsi[:])
                step(dve.tensor_scalar(ls[:, 4, 0:1], ls[:, 1, 0:1], LAM_INIT, None, ALU.add))
                step(dve.tensor_tensor(ls[:, 5, 0:1], ls[:, 1, 1:2], ls[:, 4, 0:1], ALU.subtract))
                dve.tensor_scalar(gain[:], gain[:], 1.0 - LAM_INIT, None, ALU.mult).then_inc(gain_ready, 1)

                def score(u):
                    h, i, s = u // NT, u % NT, u % SLOTS
                    if i == 0:
                        dve.wait_ge(bias_ready, h + 1)
                    if u >= SLOTS:
                        dve.wait_ge(mapT, tr_before[u - SLOTS + 1])
                    L, n, nch = width(u), qk_before[u], chunks_of(u)
                    for m in range(2):
                        for c in range(nch):
                            w = min(BANK, L - c * BANK)
                            dve.wait_ge(qk_done, n + 1)
                            x0 = c * BANK + SEQ - P - P * i
                            dve.tensor_tensor_reduce(S[:, s, m, c * BANK:c * BANK + w], bank[n % 4][:, 0:w],
                                                     bias[:, h % 2, x0:x0 + w], 1.0, -BIG, ALU.add, ALU.max,
                                                     mx[:, s, m, c:c + 1]).then_inc(scored, 1)
                            n += 1
                    dve.wait_ge(scored, n)
                    dve.tensor_reduce(nm[:, s], mx[:, s, :, 0:nch], AX.X, ALU.max, negate=True).then_inc(maxed, 1)

                def mix(u):
                    s, L = u % SLOTS, width(u)
                    dve.wait_ge(exped, 2 * (u + 1))
                    if u >= SLOTS:
                        dve.wait_ge(o_sq, u - SLOTS + 1)
                        dve.wait_ge(o_used, u - SLOTS + 1)
                    dve.reciprocal(ri[:, s], rs[:, s]).then_inc(inv_step, 1)
                    dve.wait_ge(inv_step, 2 * u + 1)
                    dve.scalar_tensor_tensor(c2[:, s], ri[:, s, 1:2], ls[:, 5, 0:1], rs[:, s, 0:1], ALU.mult, ALU.mult).then_inc(inv_step, 1)
                    dve.wait_ge(inv_step, 2 * u + 2)
                    dve.scalar_tensor_tensor(S[:, s, 0, 0:L], S[:, s, 1, 0:L], c2[:, s, 0:1], S[:, s, 0, 0:L],
                                             ALU.mult, ALU.add).then_inc(mixed, 1)

                def norm(h):
                    dve.wait_ge(o_sq, NT * (h + 1))
                    dve.tensor_scalar(oss[:, h % 2], oss[:, h % 2], 1.0 / VD, EPS, ALU.mult, ALU.add).then_inc(fin_dve, 1)
                    dve.wait_ge(fin_act, h + 1)
                    dve.reciprocal(oss[:, h % 2], oss[:, h % 2]).then_inc(fin_dve, 1)
                    dve.wait_ge(fin_dve, 3 * h + 2)
                    r = oss[:, h % 2].rearrange("p (t o) -> p t o", o=1).to_broadcast([P, NT, VD])
                    dve.tensor_tensor(o[:, h % 2], o[:, h % 2], r, ALU.mult).then_inc(fin_dve, 1)

                for n in range(UN + 1):
                    if n < UN:
                        score(n)
                    if n >= 1:
                        mix(n - 1)
                    if n in FIN_AT:
                        norm(FIN_AT.index(n))
                norm(HEADS - 1)

            @block.scalar
            def _(act):
                def exps(u):
                    s, L = u % SLOTS, width(u)
                    act.wait_ge(maxed, u + 1)
                    for m in range(2):
                        act.activation(S[:, s, m, 0:L], S[:, s, m, 0:L], ACT.Exp, bias=nm[:, s, m:m + 1],
                                       accum_out=rs[:, s, m:m + 1]).then_inc(exped, 1)

                def evacuate(u):
                    h, i = u // NT, u % NT
                    for c in range(chunks_of(u)):
                        n = tr_before[u] + c
                        w = min(BANK, width(u) - c * BANK)
                        act.wait_ge(mapT, n + 1)
                        if n >= 2:
                            act.wait_ge(pv_chunk, n - 1)
                        act.activation(aT[:, n % 2, 0:w], bank[4 + n % 2][:, 0:w], ACT.Copy).then_inc(aT_ready, 1)
                    act.wait_ge(pv_chunk, tr_before[u + 1])
                    if i == 0 and h >= 2:
                        act.wait_ge(fin_T, 4 * (h - 1))
                    act.activation(o[:, h % 2, i], bank[6 + u % 2][:, 0:VD], ACT.Copy, scale=ri[:, u % SLOTS, 0:1]).then_inc(o_used, 1)
                    if u:
                        act.wait_ge(o_sq, u)
                    act.activation(sqj[:], bank[6 + u % 2][:, 0:VD], ACT.Square, scale=ri[:, u % SLOTS, 0:1], accum_out=oss[:, h % 2, i:i + 1]).then_inc(o_sq, 1)

                def finish(h):
                    act.wait_ge(fin_dve, 3 * h + 1)
                    act.activation(oss[:, h % 2], oss[:, h % 2], ACT.Sqrt).then_inc(fin_act, 1)
                    act.wait_ge(gain_ready, 1)
                    for t in range(4):
                        act.wait_ge(fin_T, 4 * h + t + 1)
                        act.activation(oT[:, h, t * BANK:(t + 1) * BANK], bank[4 + t % 2][:], ACT.Copy,
                                       scale=gain[:, 0:1]).then_inc(fin_out, 1)

                for n in range(UN + 2):
                    if 1 <= n <= UN:
                        exps(n - 1)
                    if n >= 2:
                        evacuate(n - 2)
                    if n in FIN_AT:
                        finish(FIN_AT.index(n))
                finish(HEADS - 1)

            @block.tensor
            def _(pe):
                def qk(u):
                    h, i = u // NT, u % NT
                    if i % GRP == 0:
                        pe.wait_ge(qk_in[i // GRP], 96 * (h + 1))
                    n = qk_before[u]
                    for m in range(2):
                        for c in range(chunks_of(u)):
                            w = min(BANK, width(u) - c * BANK)
                            if n >= 4:
                                pe.wait_ge(scored, n - 3)
                            qt, cols = q[:, m, i * P:(i + 1) * P].bitcast(F32R), slice(c * BANK, c * BANK + w)
                            pe.matmul(bank[n % 4][:, 0:w], qt, kh[:, m, cols].bitcast(F32R), start=True, stop=False)
                            pe.matmul(bank[n % 4][:, 0:w], qt, kl[:, m, cols].bitcast(F32R), start=False, stop=True).then_inc(qk_done, 1)
                            n += 1

                def pv(u, c):
                    h, n = u // NT, tr_before[u] + c
                    w = min(BANK, width(u) - c * BANK) // P
                    pe.wait_ge(aT_ready, n + 1)
                    if c == 0 and u % NT == 0:
                        pe.wait_ge(v_in[h % 2], 16 * (h // 2 + 1))
                    if c == 0 and u >= 2:
                        pe.wait_ge(o_used, u - 1)
                        pe.wait_ge(o_sq, u - 1)
                    for b in range(w):
                        kt = GRP * c + b
                        last = pe.matmul(bank[6 + u % 2][:, 0:VD], aT[:, n % 2, b * P:(b + 1) * P], v[:, h % 2, kt],
                                         start=kt == 0, stop=kt == u % NT)
                    last.then_inc(pv_chunk, 1)

                def transpose_and_multiply(u):
                    pe.wait_ge(mixed, u + 1)
                    for c in range(chunks_of(u)):
                        n = tr_before[u] + c
                        if n >= 2:
                            pe.wait_ge(aT_ready, n - 1)
                        w = min(BANK, width(u) - c * BANK) // P
                        for b in range(w):
                            last = pe.transpose(bank[4 + n % 2][:, b * P:(b + 1) * P],
                                                S[:, u % SLOTS, 0, c * BANK + b * P:c * BANK + (b + 1) * P], ident[:])
                        last.then_inc(mapT, 1)
                        if c:
                            pv(u, c - 1)
                    pv(u, chunks_of(u) - 1)

                def head_T(h):
                    pe.wait_ge(fin_dve, 3 * (h + 1))
                    for t in range(4):
                        if t >= 2:
                            pe.wait_ge(fin_out, 4 * h + t - 1)
                        for b in range(4):
                            last = pe.transpose(bank[4 + t % 2][:, b * P:(b + 1) * P], o[:, h % 2, 4 * t + b], ident[:])
                        last.then_inc(fin_T, 1)
                    pe.wait_ge(fin_out, 4 * h + 4)

                for n in range(UN + 2):
                    if n < UN:
                        qk(n)
                    if n >= 2:
                        transpose_and_multiply(n - 2)
                    if n in FIN_AT:
                        head_T(FIN_AT.index(n))
                head_T(HEADS - 1)


def out_projection(nc, ident, oT, wo_first, srs, logits, a, d):
    W = NEG + NE
    with ExitStack() as ctx:
        sb = lambda name, shape, dt=F32: ctx.enter_context(nc.sbuf_tensor(name, shape, dt))
        sem = ctx.enter_context(phase_semaphores(nc))
        bank = [ctx.enter_context(nc.psum_tensor(f"d_bank{i}", [P, BANK], F32)) for i in range(8)]
        woh, wol = sb("w_out_hi", [P, KT, D], F32R), sb("w_out_lo", [P, KT, D], F32R)
        wo_second = sb("w_out_second", [P, KT, BANK])
        wo = (wo_first, wo_second)
        wo_in = sem("w_out_second_in")
        ssm = sb("ssmT_tile", [P, 2, 4, P])
        mh, ml = sb("mix_hi", [P, 2, KT, P], F32R), sb("mix_lo", [P, 2, KT, P], F32R)
        wr = sb("w_router", [P, KT, W])
        br = sb("b_router", [P, W])
        gain = sb("gain_moe", [P, D])
        x = sb("x_again", [P, 2, D])
        x1, h2 = sb("x1_tile", [P, 2, D]), sb("h2_tile", [P, 2, D])
        tmp = sb("x1_tmp", [P, 2, BANK])
        junk = sb("junk_d", [P, D])
        ss = sb("sumsq_d", [P, NT])
        h2T = sb("h2T", [P, KT, P])
        wr_in, gain_in = sem("w_router_in"), sem("gain_moe_in")
        woh_done, wol_done, mh_done, ml_done = (sem(n) for n in ("w_out_hi_done", "w_out_lo_done", "mix_hi_done", "mix_lo_done"))
        ssm_in = [sem(f"ssmT_in{i}") for i in range(2)]
        quarter = [(slice(4 * q, 4 * q + 4), slice(c * BANK, (c + 1) * BANK)) for c in range(2) for q in range(2)]
        x_in = [sem(f"x_again_in{i}") for i in range(2)]
        mm_done, tmp_done, x1_done, sq_done, rstd_step, root, h2_done = (
            sem(n) for n in ("wo_done", "tmp_done", "x1_done", "x1_sq", "rstd_d", "root_d", "h2_done"))
        h2T_psum, h2T_done, lg_done, lg_used = (sem(n) for n in ("h2T_psum", "h2T_done", "lg_done", "lg_used"))
        x1_st = [sem(f"x1_stored{i}") for i in range(2)]
        h2_st = [sem(f"h2_stored{i}") for i in range(2)]
        with nc.Block() as block:

            @block.sync
            def _(sp):
                def ssm_load(i):
                    sp.dma_start(ssm[:, i % 2], d["ssmT"][:, :, i * P:(i + 1) * P]).then_inc(ssm_in[i % 2], 16)

                ssm_load(0)
                sp.dma_start(wo_second[:], a["w_out"][0].rearrange("(k p) n -> p k n", p=P)[:, :, BANK:D]).then_inc(wo_in, 16)
                ssm_load(1)
                sp.dma_start(gain[:], a["norm_moe"].to_broadcast([P, D])).then_inc(gain_in, 16)
                sp.dma_start(wr[:, :, 0:NEG], a["w_router_group"][0].rearrange("(p k) n -> p k n", k=KT)).then_inc(wr_in, 16)
                sp.dma_start(wr[:, :, NEG:W], a["w_router_expert"][0].rearrange("(p k) n -> p k n", k=KT)).then_inc(wr_in, 16)
                sp.dma_start(br[:, 0:NEG], a["b_router_group"].to_broadcast([P, NEG])).then_inc(wr_in, 16)
                sp.dma_start(br[:, NEG:W], a["b_router_expert"].to_broadcast([P, NE])).then_inc(wr_in, 16)
                for i in range(NT + 1):
                    if i < NT:
                        if i >= 2:
                            sp.wait_ge(tmp_done, 2 * (i - 1))
                        sp.dma_start(x[:, i % 2], a["x"][0, i * P:(i + 1) * P]).then_inc(x_in[i % 2], 16)
                    if 1 <= i < NT - 1:
                        sp.wait_ge(ml_done, 2 * i)
                        ssm_load(i + 1)
                    if i:
                        t = i - 1
                        sp.wait_ge(x1_done, 2 * (t + 1))
                        sp.dma_start(d["x1"][t * P:(t + 1) * P], x1[:, t % 2]).then_inc(x1_st[t % 2], 16)
                        sp.wait_ge(h2_done, t + 1)
                        sp.dma_start(d["h2"][t * P:(t + 1) * P], h2[:, t % 2]).then_inc(h2_st[t % 2], 16)
                for s in range(2):
                    sp.wait_ge(x1_st[s], 16 * NT // 2)
                    sp.wait_ge(h2_st[s], 16 * NT // 2)

            @block.scalar
            def _(act):
                def mix_hi(i):
                    if i >= 2:
                        act.wait_ge(mm_done, 2 * (i - 1))
                    act.activation(mh[:, i % 2, 0:4], oT[:, :, i * P:(i + 1) * P], ACT.Copy).then_inc(mh_done, 1)
                    act.wait_ge(ssm_in[i % 2], 16 * (i // 2 + 1))
                    act.activation(mh[:, i % 2, 4:KT], ssm[:, i % 2], ACT.Copy).then_inc(mh_done, 1)

                mix_hi(0)
                mix_hi(1)
                for n, (ks, cols) in enumerate(quarter):
                    if n == 2:
                        act.wait_ge(wo_in, 16)
                    act.activation(woh[:, ks, cols], wo[n // 2][:, ks], ACT.Copy).then_inc(woh_done, 1)

                def h2_out(t):
                    for h in range(2):
                        act.wait_ge(h2T_psum, 2 * t + h + 1)
                        if t and h == 0:
                            act.wait_ge(lg_done, t)
                        act.activation(h2T[:, 4 * h:4 * h + 4], bank[4 + h][:].rearrange("p (k t) -> p k t", k=4), ACT.Copy
                                       ).then_inc(h2T_done, 1)
                for i in range(NT):
                    act.wait_ge(x1_done, 2 * (i + 1))
                    if i:
                        act.wait_ge(sq_done, i)
                    act.activation(junk[:], x1[:, i % 2], ACT.Square, accum_out=ss[:, i:i + 1]).then_inc(sq_done, 1)
                    act.wait_ge(rstd_step, 2 * i + 1)
                    act.activation(ss[:, i:i + 1], ss[:, i:i + 1], ACT.Sqrt).then_inc(root, 1)
                    if i + 2 < NT:
                        mix_hi(i + 2)
                    h2_out(i)

            @block.vector
            def _(dve):
                def router(t):
                    dve.wait_ge(lg_done, t + 1)
                    dve.tensor_tensor(logits[:, t], bank[6 + t % 2][:, 0:W], br[:], ALU.add).then_inc(lg_used, 1)

                def mix_lo(i):
                    dve.wait_ge(mh_done, 2 * i + 1)
                    dve.tensor_tensor(ml[:, i % 2, 0:4], oT[:, :, i * P:(i + 1) * P], mh[:, i % 2, 0:4], ALU.subtract).then_inc(ml_done, 1)
                    dve.wait_ge(mh_done, 2 * i + 2)
                    dve.tensor_tensor(ml[:, i % 2, 4:KT], ssm[:, i % 2], mh[:, i % 2, 4:KT], ALU.subtract).then_inc(ml_done, 1)

                mix_lo(0)
                mix_lo(1)
                for n, (ks, cols) in enumerate(quarter):
                    dve.wait_ge(woh_done, n + 1)
                    dve.tensor_tensor(wol[:, ks, cols], wo[n // 2][:, ks], woh[:, ks, cols], ALU.subtract).then_inc(wol_done, 1)
                dve.wait_ge(gain_in, 16)
                dve.wait_ge(wr_in, 64)
                for i in range(NT):
                    dve.wait_ge(x_in[i % 2], 16 * (i // 2 + 1))
                    if i >= 2:
                        dve.wait_ge(x1_st[i % 2], 16 * (i // 2))
                    for h in range(2):
                        cols = slice(h * BANK, (h + 1) * BANK)
                        dve.wait_ge(mm_done, 2 * i + h + 1)
                        if 2 * i + h >= 2:
                            dve.wait_ge(x1_done, 2 * i + h - 1)
                        dve.scalar_tensor_tensor(tmp[:, h], bank[2 * h + 1][:], srs[:, i:i + 1], x[:, i % 2, cols],
                                                 ALU.mult, ALU.add).then_inc(tmp_done, 1)
                        dve.wait_ge(tmp_done, 2 * i + h + 1)
                        dve.tensor_tensor(x1[:, i % 2, cols], bank[2 * h][:], tmp[:, h], ALU.add).then_inc(x1_done, 1)
                    dve.wait_ge(sq_done, i + 1)
                    dve.tensor_scalar(ss[:, i:i + 1], ss[:, i:i + 1], 1.0 / D, EPS, ALU.mult, ALU.add).then_inc(rstd_step, 1)
                    dve.wait_ge(root, i + 1)
                    dve.reciprocal(ss[:, i:i + 1], ss[:, i:i + 1]).then_inc(rstd_step, 1)
                    dve.wait_ge(rstd_step, 2 * i + 2)
                    if i >= 2:
                        dve.wait_ge(h2_st[i % 2], 16 * (i // 2))
                        dve.wait_ge(h2T_psum, 2 * (i - 1))
                    dve.scalar_tensor_tensor(h2[:, i % 2], x1[:, i % 2], ss[:, i:i + 1], gain[:], ALU.mult, ALU.mult).then_inc(h2_done, 1)
                    if i + 2 < NT:
                        mix_lo(i + 2)
                    if i:
                        router(i - 1)
                router(NT - 1)
                dve.wait_ge(lg_used, NT)

            @block.tensor
            def _(pe):
                def h2_T(t):
                    pe.wait_ge(h2_done, t + 1)
                    for h in range(2):
                        if t:
                            pe.wait_ge(h2T_done, 2 * t + h - 1)
                        for k in range(4):
                            last = pe.transpose(bank[4 + h][:, k * P:(k + 1) * P], h2[:, t % 2, 4 * h + k:D:KT], ident[:])
                        last.then_inc(h2T_psum, 1)

                def router(t):
                    pe.wait_ge(h2T_done, 2 * t + 2)
                    if t >= 2:
                        pe.wait_ge(lg_used, t - 1)
                    for k in range(KT):
                        last = pe.matmul(bank[6 + t % 2][:, 0:W], h2T[:, k], wr[:, k], start=k == 0, stop=k == KT - 1)
                    last.then_inc(lg_done, 1)

                pe.wait_ge(wr_in, 64)
                for i in range(NT):
                    pe.wait_ge(mh_done, 2 * i + 2)
                    pe.wait_ge(ml_done, 2 * i + 2)
                    for h in range(2):
                        cols = slice(h * BANK, (h + 1) * BANK)
                        if i:
                            pe.wait_ge(x1_done, 2 * i + h - 1)
                        for q in range(2):
                            if i == 0:
                                pe.wait_ge(wol_done, 2 * h + q + 1)
                            if i and h == 1 and q == 1:
                                h2_T(i - 1)
                            for k in range(4 * q, 4 * q + 4):
                                o = bank[2 * h + q][:]
                                pe.matmul(o, mh[:, i % 2, k], woh[:, k, cols], start=k == 4 * q, stop=False)
                                pe.matmul(o, mh[:, i % 2, k], wol[:, k, cols], start=False, stop=False)
                                last = pe.matmul(o, ml[:, i % 2, k], woh[:, k, cols], start=False, stop=k == 4 * q + 3)
                        last.then_inc(mm_done, 1)
                    if i:
                        router(i - 1)
                h2_T(NT - 1)
                router(NT - 1)


def route(nc, ident, ones, logits, gates, dest, ids, meta, d):
    W = NEG + NE
    with ExitStack() as ctx:
        sb = lambda name, shape, dt=F32: ctx.enter_context(nc.sbuf_tensor(name, shape, dt))
        sem = ctx.enter_context(phase_semaphores(nc))
        bank = [ctx.enter_context(nc.psum_tensor(f"r_bank{i}", [P, BANK], F32)) for i in range(3)]
        count_i, count = sb("count_i", [P, P], I32), sb("count", [P, P])
        tri = sb("earlier", [P, P])
        thr = sb("block_edges", [P, NT])
        tok = sb("token_id", [P, NT], I32)
        zero = sb("zero_ids", [NBLK, P], I32)
        t1 = lambda n: sb(n, [P, NT, 1])
        gmax, gidx, gsum, m1, m2, i1, i2, esum = (t1(n) for n in ("gmax", "gidx", "gsum", "m1", "m2", "i1", "i2", "esum"))
        g_eq, goh, gex = (sb(n, [P, NT, NEG]) for n in ("g_eq", "g_onehot", "g_exp"))
        ein, etmp, oh1, oh2, eex = (sb(n, [P, NT, EPG]) for n in ("e_in", "e_tmp", "onehot1", "onehot2", "e_exp"))
        p2 = t1("p2")
        A = sb("assigned", [P, 2, NT, NEG, EPG])
        M = sb("assigned_any", [P, NT, NE])
        base = sb("rank_base", [P, NT + 1, NE])
        big = sb("compare", [P, NBLK, NE])
        nblk, pend, sbase, rank = sb("n_blocks", [P, NE]), sb("block_end", [P, NE]), sb("slot_base", [P, NE]), sb("rank", [P, NT, NE])
        df, bf = sb("dest_f", [P, NT, 1]), sb("meta_f", [P, META])
        filled, order = sb("filled", [P, NE]), sb("filled_order", [P, NE])
        idf = sb("ids_f", [NBLK, P])
        idi = sb("ids_i", [NBLK, P], I32)
        c_step, c_ready, r_step, exp_in, exp_done, any_ready, pref_done = (
            sem(n) for n in ("c_step", "c_ready", "r_step", "exp_in", "exp_done", "any_ready", "pref_done"))
        zero_st, dest_ready, scattered, ids_in, ids_f, ids_T = (
            sem(n) for n in ("zero_stored", "dest_ready", "scattered", "ids_loaded", "ids_f_ready", "ids_T"))
        with nc.Block() as block:

            @block.gpsimd
            def _(pool):
                pool.iota(count_i[:], pattern=[[1, P]], base=0, channel_multiplier=0).then_inc(c_step, 1)
                pool.iota(tok[:], pattern=[[P, NT]], base=0, channel_multiplier=1).then_inc(c_step, 1)
                pool.memset(zero[:], 0).then_inc(c_step, 1)
                pool.memset(ids[:], 0).then_inc(c_step, 1)
                pool.wait_ge(c_step, 4)
                pool.tensor_copy(count[:], count_i[:]).then_inc(c_step, 1)
                pool.wait_ge(c_step, 5)
                pool.tensor_scalar(thr[:], count[:, 0:NT], float(P), None, ALU.mult).then_inc(c_ready, 1)
                pool.affine_select(out=tri[:], in_=ones[:], pattern=[[1, P]], compare_op=ALU.is_gt, fill=0.0,
                                   base=0, channel_multiplier=-1).then_inc(c_ready, 1)
                pool.wait_ge(zero_st, 16)
                pool.wait_ge(dest_ready, 2)
                for k in range(2):
                    for i in range(NT):
                        pool.indirect_dma_start(d["slot_token"], bass.IndirectOffsetOnAxis(ap=dest[:, k, i:i + 1], axis=0),
                                                tok[:, i:i + 1], None).then_inc(scattered, 16)
                pool.wait_ge(scattered, 16 * 2 * NT)

            @block.sync
            def _(sp):
                sp.wait_ge(c_step, 3)
                sp.dma_start(d["slot_token"].rearrange("(b p) o -> b (p o)", p=P), zero[:]).then_inc(zero_st, 16)
                sp.wait_ge(scattered, 16 * 2 * NT)
                sp.dma_start(idi[:], d["slot_token"].rearrange("(b p) o -> b (p o)", p=P)).then_inc(ids_in, 16)

            @block.scalar
            def _(act):
                act.wait_ge(exp_in, 1)
                act.activation(gex[:], gex[:], ACT.Exp).then_inc(exp_done, 1)
                act.wait_ge(exp_in, 3)
                act.activation(eex[:], eex[:], ACT.Exp).then_inc(exp_done, 1)
                act.activation(p2[:], p2[:], ACT.Exp).then_inc(exp_done, 1)

            @block.tensor
            def _(pe):
                pe.wait_ge(c_ready, 2)
                pe.wait_ge(any_ready, 1)
                m = M[:].rearrange("p t e -> p (t e)")
                pe.matmul(bank[0][:], tri[:], m, start=True, stop=True)
                pe.matmul(bank[1][:], ones[:], m, start=True, stop=True).then_inc(pref_done, 1)
                pe.wait_ge(ids_f, 1)
                pe.transpose(bank[2][:, 0:NBLK], idf[:], ident[0:NBLK, 0:NBLK]).then_inc(ids_T, 1)

            @block.vector
            def _(dve):
                step = Step(dve, r_step)
                Lg, Le = logits[:, :, 0:NEG], logits[:, :, NEG:W]
                wide = lambda t, n: t.to_broadcast([P, NT, n])
                dve.wait_ge(c_ready, 2)

                def first_max(val, n, mxt, idx, out, tmp):
                    step(dve.tensor_reduce(mxt[:], val, AX.X, ALU.max))
                    step(dve.tensor_tensor(tmp[:], val, wide(mxt[:], n), ALU.is_ge))
                    cnt = count[:, 0:n].rearrange("p (o n) -> p o n", o=1).to_broadcast([P, NT, n])
                    step(dve.scalar_tensor_tensor(tmp[:], tmp[:], -64.0, cnt, ALU.mult, ALU.add))
                    step(dve.tensor_reduce(idx[:], tmp[:], AX.X, ALU.min))
                    step(dve.tensor_tensor(out[:], tmp[:], wide(idx[:], n), ALU.is_equal))

                first_max(Lg, NEG, gmax, gidx, goh, g_eq)
                dve.tensor_tensor(gex[:], Lg, wide(gmax[:], NEG), ALU.subtract).then_inc(exp_in, 1)
                for g in range(NEG):
                    o = wide(goh[:, :, g:g + 1], EPG)
                    e = Le[:, :, g * EPG:(g + 1) * EPG]
                    if g == 0:
                        step(dve.tensor_tensor(ein[:], e, o, ALU.mult))
                    else:
                        step(dve.tensor_tensor(etmp[:], e, o, ALU.mult))
                        step(dve.tensor_tensor(ein[:], ein[:], etmp[:], ALU.add))
                first_max(ein[:], EPG, m1, i1, oh1, etmp)
                dve.tensor_tensor(eex[:], ein[:], wide(m1[:], EPG), ALU.subtract).then_inc(exp_in, 1)
                dve.wait_ge(exp_in, 2)
                step(dve.scalar_tensor_tensor(ein[:], oh1[:], -BIG, ein[:], ALU.mult, ALU.add))
                first_max(ein[:], EPG, m2, i2, oh2, etmp)
                dve.tensor_tensor(p2[:], m2[:], m1[:], ALU.subtract).then_inc(exp_in, 1)
                for k, oh in enumerate((oh1, oh2)):
                    g4 = goh[:].rearrange("p t (g o) -> p t g o", o=1).to_broadcast([P, NT, NEG, EPG])
                    e4 = oh[:].rearrange("p t (o e) -> p t o e", o=1).to_broadcast([P, NT, NEG, EPG])
                    step(dve.tensor_tensor(A[:, k], g4, e4, ALU.mult))
                Ak = [A[:, k].rearrange("p t g e -> p t (g e)") for k in range(2)]
                dve.tensor_tensor(M[:], Ak[0], Ak[1], ALU.add).then_inc(any_ready, 1)
                dve.wait_ge(exp_done, 3)
                step(dve.tensor_reduce(gsum[:], gex[:], AX.X, ALU.add))
                step(dve.tensor_reduce(esum[:], eex[:], AX.X, ALU.add))
                step(dve.tensor_tensor(gsum[:], gsum[:], esum[:], ALU.mult))
                step(dve.reciprocal(gates[:, 0], gsum[:, :, 0]))
                step(dve.tensor_tensor(gates[:, 1], gates[:, 0], p2[:, :, 0], ALU.mult))
                dve.wait_ge(pref_done, 1)
                tot = bank[1][:].rearrange("p (t e) -> p t e", e=NE)
                step(dve.memset(base[:, 0], 0.0))
                for i in range(NT):
                    step(dve.tensor_tensor(base[:, i + 1], base[:, i], tot[:, i], ALU.add))
                cmp1 = big[:].rearrange("p b e -> p (b e)")[:, 0:NE * NT].rearrange("p (e j) -> p e j", j=NT)
                step(dve.tensor_tensor(cmp1, base[:, NT].rearrange("p (e o) -> p e o", o=1).to_broadcast([P, NE, NT]),
                                       thr[:].rearrange("p (o j) -> p o j", o=1).to_broadcast([P, NE, NT]), ALU.is_gt))
                step(dve.tensor_reduce(nblk[:], cmp1, AX.X, ALU.add))
                step(dve.tensor_tensor_scan(pend[:], ones[:, 0:NE], nblk[:], 0.0, ALU.mult, ALU.add))
                step(dve.tensor_tensor(sbase[:], pend[:], nblk[:], ALU.subtract))
                step(dve.tensor_scalar(sbase[:], sbase[:], float(P), None, ALU.mult))
                step(dve.tensor_tensor(rank[:], base[:, 0:NT], bank[0][:].rearrange("p (t e) -> p t e", e=NE), ALU.add))
                step(dve.tensor_tensor(rank[:], rank[:], sbase[:].rearrange("p (o e) -> p o e", o=1).to_broadcast([P, NT, NE]), ALU.add))
                for k in range(2):
                    step(dve.tensor_tensor(M[:], Ak[k], rank[:], ALU.mult))
                    step(dve.tensor_reduce(df[:], M[:], AX.X, ALU.add))
                    dve.tensor_copy(dest[:, k], df[:, :, 0]).then_inc(dest_ready, 1)
                    dve.wait_ge(dest_ready, k + 1)
                over = lambda t, n: t[:].rearrange("p (o e) -> p o e", o=1).to_broadcast([P, n, NE])
                upto = lambda n: count[:, 0:n].rearrange("p (b o) -> p b o", o=1).to_broadcast([P, n, NE])
                step(dve.tensor_scalar(filled[:], nblk[:], 0.0, None, ALU.is_gt))
                step(dve.tensor_tensor_scan(order[:], ones[:, 0:NE], filled[:], 0.0, ALU.mult, ALU.add))
                step(dve.tensor_tensor(big[:], over(pend, NBLK), upto(NBLK), ALU.is_le))
                step(dve.tensor_tensor(big[:], big[:], over(filled, NBLK), ALU.mult))
                step(dve.tensor_reduce(bf[:, 0:NBLK], big[:], AX.X, ALU.add))
                step(dve.tensor_copy(bf[:, META_BLOCKS:META_BLOCKS + 1], pend[:, NE - 1:NE]))
                step(dve.tensor_copy(bf[:, META_EXPERTS:META], order[:, NE - 1:NE]))
                step(dve.tensor_scalar(df[:, 0], order[:, NE - 1:NE], -1.0, None, ALU.add))
                step(dve.tensor_scalar(bf[:, 0:NBLK], bf[:, 0:NBLK], df[:, 0, 0:1], None, ALU.min))
                step(dve.tensor_tensor(big[:, 0:NE], over(order, NE), upto(NE), ALU.is_le))
                step(dve.tensor_reduce(bf[:, META_ID:META_ID + NE], big[:, 0:NE], AX.X, ALU.add))
                step(dve.tensor_copy(meta[:], bf[:]))
                dve.wait_ge(ids_in, 16)
                dve.tensor_copy(idf[:], idi[:]).then_inc(ids_f, 1)
                dve.wait_ge(ids_T, 1)
                step(dve.tensor_copy(ids[:, 0:NBLK], bank[2][:, 0:NBLK]))


def experts(nc, ident, ones, ids, meta, a, d):
    with ExitStack() as ctx:
        sb = lambda name, shape, dt=F32: ctx.enter_context(nc.sbuf_tensor(name, shape, dt))
        sem = ctx.enter_context(phase_semaphores(nc))
        bank = [ctx.enter_context(nc.psum_tensor(f"m_bank{i}", [P, BANK], F32)) for i in range(7)]
        G, U, XT, HT, DN = bank[0], bank[1], bank[2:4], bank[4], bank[5:7]
        FT = FF // P
        N_W = KT * FF
        HW = N_W // 2
        raw = [sb(f"w_{n}_raw", [P, N_W]) for n in ("gate", "up", "down")]
        whi = [sb(f"w_{n}_hi", [P, N_W], F32R) for n in ("gate", "up", "down")]
        wlo = [sb(f"w_{n}_lo", [P, N_W], F32R) for n in ("gate", "up", "down")]
        idx = sb("idx", [P, 1], I32)
        spare, hold, last_copy = sb("spare", [P, 16]), sb("hold", [P, 1]), sb("last_copy", [P, 1])
        x = sb("rows_in", [P, D])
        xh, xl = sb("rows_T_hi", [P, KT, P], F32R), sb("rows_T_lo", [P, KT, P], F32R)
        sil, hid = sb("silu", [P, FF]), sb("hidden", [P, FF])
        hh, hl = sb("hidden_T_hi", [P, FT, P], F32R), sb("hidden_T_lo", [P, FT, P], F32R)
        out = sb("rows_out", [P, D])
        w_in = [sem(f"w_{n}_in") for n in ("gate", "up", "down")]
        hi_done = [sem(f"w_{n}_hi_done") for n in ("gate", "up", "down")]
        lo_done = [sem(f"w_{n}_lo_done") for n in ("gate", "up", "down")]
        x_in, out_st = sem("rows_in_s"), sem("rows_stored")
        g_done, u_done, d_done, silu_done, hid_done, idx_set = (sem(n) for n in ("g_done", "u_done", "d_done", "silu_done", "hid_done", "idx_set"))
        xT_psum, xh_done, xl_done, hT_psum, hh_done, hl_done, d_used0, d_used1, primed = (
            sem(n) for n in ("rT_psum", "rT_hi_done", "rT_lo_done", "hidT_psum", "hidT_hi_done", "hidT_lo_done",
                             "d_used0", "d_used1", "primed"))
        with nc.Block() as block:

            @block.vector
            def _(dve):
                dve.memset(out[:], 0.0).then_inc(primed, 1)
                start = [(silu_done, 1), (hid_done, 1), (hh_done, 1), (hl_done, 1), (d_used0, 1), (d_used1, 1)]
                start += [(s, 2) for s in hi_done + lo_done]
                for n, (s, times) in enumerate(start):
                    dve.memset(spare[:, n:n + 1], 0.0).then_inc(s, times)

            @block.scalar
            def _(act):
                act.wait_ge(primed, 1)
                act.dma_start(d["rows"][NBLK], out[:]).then_inc(out_st, 16)

        with nc.Block() as block:
            blocks = lambda eng: eng.value_load(meta[0:1, META_BLOCKS:META_BLOCKS + 1], min_val=1, max_val=NBLK - 1)
            place = lambda eng, b: eng.value_load(meta[0:1, bass.ds(b, 1)], min_val=0, max_val=NE - 1)
            halves = [slice(0, HW), slice(HW, N_W)]

            @block.sync
            def _(sp):
                n = sp.value_load(meta[0:1, META_EXPERTS:META_EXPERTS + 1], min_val=1, max_val=NE)
                with sp.Fori(0, n) as o:
                    e = sp.value_load(meta[0:1, bass.ds(META_ID + o, 1)], min_val=0, max_val=NE - 1)
                    for w, name in enumerate(("w_gate", "w_up", "w_down")):
                        k = FT if name == "w_down" else KT
                        sp.wait_ge(hi_done[w], 2 * o + 2)
                        sp.wait_ge(lo_done[w], 2 * o + 2)
                        sp.dma_start(raw[w][:], a[name][0, bass.ds(e, 1)].rearrange("o (p k) n -> p (o k n)", k=k)).then_inc(w_in[w], 16)

            @block.gpsimd
            def _(pool):
                pool.tensor_copy(idx[:], ids[:, 0:1]).then_inc(idx_set, 1)
                pool.wait_ge(idx_set, 1)
                pool.indirect_dma_start(x[:], None, d["h2"], bass.IndirectOffsetOnAxis(ap=idx[:], axis=0)).then_inc(x_in, 16)
                with pool.Fori(0, blocks(pool)) as b:
                    pool.wait_ge(xT_psum, 2 * b + 2)
                    pool.tensor_copy(idx[:], ids[:, bass.ds(b + 1, 1)]).then_inc(idx_set, 1)
                    pool.wait_ge(idx_set, b + 2)
                    pool.tensor_tensor(hold[:], ones[:, 0:1], ones[:, 1:2], ALU.add)
                    pool.indirect_dma_start(x[:], None, d["h2"], bass.IndirectOffsetOnAxis(ap=idx[:], axis=0)).then_inc(x_in, 16)

            @block.scalar
            def _(act):
                def split_hi(w, order, which=(0, 1)):
                    act.wait_ge(w_in[w], 16 * order + 16)
                    for s in (halves[i] for i in which):
                        act.activation(whi[w][:, s], raw[w][:, s], ACT.Copy).then_inc(hi_done[w], 1)

                def rows_hi(h, want):
                    act.wait_ge(xT_psum, want)
                    act.activation(xh[:, 4 * h:4 * h + 4], XT[h][:].rearrange("p (k t) -> p k t", k=4), ACT.Copy).then_inc(xh_done, 1)

                for w in range(3):
                    split_hi(w, 0)
                rows_hi(0, 1)
                rows_hi(1, 2)
                with act.Fori(0, blocks(act)) as b:
                    now, order = place(act, b), place(act, b + 1)
                    with where_below(nc, act, now, order):
                        act.wait_ge(g_done, b + 1)
                        split_hi(0, order, (0,))
                    act.wait_ge(g_done, b + 1)
                    act.wait_ge(hid_done, b + 1)
                    act.activation(sil[:], G[:], ACT.Silu).then_inc(silu_done, 1)
                    with where_below(nc, act, now, order):
                        split_hi(0, order, (1,))
                    rows_hi(0, 2 * b + 3)
                    act.wait_ge(hT_psum, b + 1)
                    act.activation(hh[:], HT[:].rearrange("p (k t) -> p k t", k=FT), ACT.Copy).then_inc(hh_done, 1)
                    rows_hi(1, 2 * b + 4)
                    with where_below(nc, act, now, order):
                        split_hi(1, order)
                    act.wait_ge(d_done, 2 * b + 1)
                    act.wait_ge(out_st, 16 * b + 16)
                    act.activation(out[:, 0:BANK], DN[0][:], ACT.Copy).then_inc(d_used0, 1)
                    with where_below(nc, act, now, order):
                        act.wait_ge(d_done, 2 * b + 2)
                        split_hi(2, order)
                    act.wait_ge(d_used0, b + 2)
                    act.wait_ge(d_used1, b + 2)
                    act.dma_start(d["rows"][bass.ds(b, 1)].rearrange("o p n -> p (o n)"), out[:]).then_inc(out_st, 16)
                n = blocks(act)
                act.wait_ge(out_st, 16 * n + 16)
                act.activation(last_copy[:], ones[:, 0:1], ACT.Copy)

            @block.vector
            def _(dve):
                def split_lo(w, want, which=(0, 1)):
                    for i in which:
                        s = halves[i]
                        dve.wait_ge(hi_done[w], want + i)
                        dve.tensor_tensor(wlo[w][:, s], raw[w][:, s], whi[w][:, s], ALU.subtract).then_inc(lo_done[w], 1)

                def rows_lo(h, want):
                    dve.wait_ge(xh_done, want)
                    dve.tensor_tensor(xl[:, 4 * h:4 * h + 4], XT[h][:].rearrange("p (k t) -> p k t", k=4), xh[:, 4 * h:4 * h + 4],
                                      ALU.subtract).then_inc(xl_done, 1)

                for w in range(3):
                    split_lo(w, 3)
                rows_lo(0, 1)
                rows_lo(1, 2)
                with dve.Fori(0, blocks(dve)) as b:
                    now, order = place(dve, b), place(dve, b + 1)
                    with where_below(nc, dve, now, order):
                        dve.wait_ge(g_done, b + 1)
                        split_lo(0, 2 * order + 3, (0,))
                    dve.wait_ge(u_done, b + 1)
                    dve.wait_ge(silu_done, b + 2)
                    dve.tensor_tensor(hid[:], sil[:], U[:], ALU.mult).then_inc(hid_done, 1)
                    dve.wait_ge(hh_done, b + 2)
                    dve.tensor_tensor(hl[:], HT[:].rearrange("p (k t) -> p k t", k=FT), hh[:], ALU.subtract).then_inc(hl_done, 1)
                    rows_lo(0, 2 * b + 3)
                    rows_lo(1, 2 * b + 4)
                    with where_below(nc, dve, now, order):
                        split_lo(0, 2 * order + 3, (1,))
                        split_lo(1, 2 * order + 3)
                    dve.wait_ge(d_done, 2 * b + 2)
                    dve.wait_ge(out_st, 16 * b + 16)
                    dve.tensor_copy(out[:, BANK:D], DN[1][:]).then_inc(d_used1, 1)
                    with where_below(nc, dve, now, order):
                        split_lo(2, 2 * order + 3)

            @block.tensor
            def _(pe):
                def rows_T(h):
                    for k in range(4):
                        last = pe.transpose(XT[h][:, k * P:(k + 1) * P], x[:, 4 * h + k:D:KT], ident[:])
                    last.then_inc(xT_psum, 1)

                def product(to, w, done):
                    for k in range(KT):
                        c = slice(k * FF, (k + 1) * FF)
                        pe.matmul(to[:], xh[:, k], whi[w][:, c], start=k == 0, stop=False)
                        pe.matmul(to[:], xh[:, k], wlo[w][:, c], start=False, stop=False)
                        last = pe.matmul(to[:], xl[:, k], whi[w][:, c], start=False, stop=k == KT - 1)
                    last.then_inc(done, 1)

                pe.wait_ge(x_in, 16)
                rows_T(0)
                rows_T(1)
                with pe.Fori(0, blocks(pe)) as b:
                    order = place(pe, b)
                    pe.wait_ge(xh_done, 2 * b + 2)
                    pe.wait_ge(xl_done, 2 * b + 2)
                    pe.wait_ge(silu_done, b + 1)
                    pe.wait_ge(hi_done[0], 2 * order + 4)
                    pe.wait_ge(lo_done[0], 2 * order + 4)
                    product(G, 0, g_done)
                    pe.wait_ge(hid_done, b + 1)
                    pe.wait_ge(hi_done[1], 2 * order + 4)
                    pe.wait_ge(lo_done[1], 2 * order + 4)
                    product(U, 1, u_done)
                    pe.wait_ge(x_in, 16 * b + 32)
                    rows_T(0)
                    pe.wait_ge(hid_done, b + 2)
                    pe.wait_ge(hh_done, b + 1)
                    pe.wait_ge(hl_done, b + 1)
                    for k in range(FT):
                        last = pe.transpose(HT[:, k * P:(k + 1) * P], hid[:, k:FF:FT], ident[:])
                    last.then_inc(hT_psum, 1)
                    rows_T(1)
                    pe.wait_ge(hh_done, b + 2)
                    pe.wait_ge(hi_done[2], 2 * order + 4)
                    pe.wait_ge(lo_done[2], 2 * order + 4)
                    pe.wait_ge(d_used0, b + 1)
                    pe.wait_ge(d_used1, b + 1)
                    for h in range(2):
                        part = lambda k: slice(k * D + h * BANK, k * D + (h + 1) * BANK)
                        for k in range(FT):
                            pe.matmul(DN[h][:], hh[:, k], whi[2][:, part(k)], start=k == 0, stop=False)
                            pe.matmul(DN[h][:], hh[:, k], wlo[2][:, part(k)], start=False, stop=False)
                        if h == 0:
                            pe.wait_ge(hl_done, b + 2)
                        for k in range(FT):
                            last = pe.matmul(DN[h][:], hl[:, k], whi[2][:, part(k)], start=False, stop=k == FT - 1)
                        last.then_inc(d_done, 1)


def combine(nc, gates, dest, a, d, out):
    R = 5
    with ExitStack() as ctx:
        sb = lambda name, shape, dt=F32: ctx.enter_context(nc.sbuf_tensor(name, shape, dt))
        sem = ctx.enter_context(phase_semaphores(nc))
        r = sb("expert_rows", [P, R, 2, D])
        x1, y = sb("x1_back", [P, R, D]), sb("y_tile", [P, R, D])
        junk = sb("junk_f", [P, D])
        gain = sb("gain_final", [P, D])
        ss = sb("sumsq_f", [P, NT])
        x_in = [sem(f"x1_back_in{i}") for i in range(R)]
        r_in = [sem(f"expert_rows_in{i}") for i in range(R)]
        st = [sem(f"out_stored{i}") for i in range(R)]
        gain_in, mix0, mix1, sq, rstd_step, root, normed = (
            sem(n) for n in ("gain_final_in", "mix_0", "mix_1", "sq_f", "rstd_f", "root_f", "normed_f"))
        with nc.Block() as block:

            @block.gpsimd
            def _(pool):
                for i in range(NT):
                    if i >= R:
                        pool.wait_ge(mix1, i - R + 1)
                    for k in range(2):
                        pool.indirect_dma_start(r[:, i % R, k], None, d["rows"].rearrange("b p n -> (b p) n"),
                                                bass.IndirectOffsetOnAxis(ap=dest[:, k, i:i + 1], axis=0)).then_inc(r_in[i % R], 16)

            @block.sync
            def _(sp):
                sp.dma_start(gain[:], a["norm_final"].rearrange("(o n) -> o n", o=1).to_broadcast([P, D])).then_inc(gain_in, 16)
                for i in range(NT + R - 1):
                    if i < NT:
                        if i >= R:
                            sp.wait_ge(mix0, i - R + 1)
                        sp.dma_start(x1[:, i % R], d["x1"][i * P:(i + 1) * P]).then_inc(x_in[i % R], 16)
                    if i >= R - 1:
                        t = i - R + 1
                        sp.wait_ge(normed, t + 1)
                        sp.dma_start(out[0, t * P:(t + 1) * P], y[:, t % R]).then_inc(st[t % R], 16)
                for s in range(R):
                    sp.wait_ge(st[s], 16 * len(range(s, NT, R)))

            @block.scalar
            def _(act):
                for i in range(NT):
                    act.wait_ge(mix1, i + 1)
                    if i:
                        act.wait_ge(sq, i)
                    act.activation(junk[:], y[:, i % R], ACT.Square, accum_out=ss[:, i:i + 1]).then_inc(sq, 1)
                    act.wait_ge(rstd_step, 2 * i + 1)
                    act.activation(ss[:, i:i + 1], ss[:, i:i + 1], ACT.Sqrt).then_inc(root, 1)

            @block.vector
            def _(dve):
                def mix(i):
                    dve.wait_ge(x_in[i % R], 16 * (i // R + 1))
                    dve.wait_ge(r_in[i % R], 32 * (i // R + 1))
                    if i >= R:
                        dve.wait_ge(st[i % R], 16 * (i // R))
                    dve.scalar_tensor_tensor(y[:, i % R], r[:, i % R, 0], gates[:, 0, i:i + 1], x1[:, i % R], ALU.mult, ALU.add).then_inc(mix0, 1)
                    dve.wait_ge(mix0, i + 1)
                    dve.scalar_tensor_tensor(y[:, i % R], r[:, i % R, 1], gates[:, 1, i:i + 1], y[:, i % R], ALU.mult, ALU.add).then_inc(mix1, 1)

                dve.wait_ge(gain_in, 16)
                mix(0)
                for i in range(NT):
                    if i + 1 < NT:
                        mix(i + 1)
                    dve.wait_ge(sq, i + 1)
                    dve.tensor_scalar(ss[:, i:i + 1], ss[:, i:i + 1], 1.0 / D, EPS, ALU.mult, ALU.add).then_inc(rstd_step, 1)
                    dve.wait_ge(root, i + 1)
                    dve.reciprocal(ss[:, i:i + 1], ss[:, i:i + 1]).then_inc(rstd_step, 1)
                    dve.wait_ge(rstd_step, 2 * i + 2)
                    dve.scalar_tensor_tensor(y[:, i % R], y[:, i % R], ss[:, i:i + 1], gain[:], ALU.mult, ALU.mult).then_inc(normed, 1)


def hybrid_layer(nc, a, out):
    dram = lambda name, shape, dt=F32: nc.dram_tensor(name, shape, dt, kind="Internal").ap()
    d = {
        "u": dram("u_d", [2, CH, P, SW]), "v": dram("v_d", [SEQ, SW]),
        "qT": dram("qT_d", [2, HEADS, P, SEQ]), "kT": dram("kT_d", [2, HEADS, P, SEQ]),
        "w1": dram("w1_d", [NB, P, GB, P]), "w2": dram("w2_d", [NB, P, GB, P]),
        "q": dram("q_d", [NB, P, GB, CH, GC]), "q2": dram("q2_d", [NB, P, GB, CH, GC]),
        "cos": dram("cos_d", [NB, P, GB, NCH]), "sin": dram("sin_d", [NB, P, GB, NCH]),
        "slot_token": dram("slot_token_d", [NBLK * P, 1], I32), "rows": dram("rows_d", [NBLK + 2, P, D]),
        "x1": dram("x1_d", [SEQ, D]), "h2": dram("h2_d", [SEQ, D]),
        "ssmT": dram("ssmT_d", [P, 4, SEQ]), "taps": dram("taps_d", [CH, GC, NG, GC]),
    }
    with ExitStack() as ctx:
        sem = ctx.enter_context(phase_semaphores(nc))
        ident = ctx.enter_context(nc.sbuf_tensor("ident", [P, P], F32))
        r8 = ctx.enter_context(nc.sbuf_tensor("r8", [P, NG], F32))
        ident_step = sem("ident_step")
        with nc.Block() as block:
            @block.gpsimd
            def _(pool):
                pool.memset(ident[:], 0.0).then_inc(ident_step, 1)
                pool.wait_ge(ident_step, 1)
                pool.affine_select(out=ident[:], in_=ident[:], pattern=[[-1, P]], compare_op=ALU.not_equal, fill=1.0,
                                   base=0, channel_multiplier=1).then_inc(ident_step, 1)
                pool.wait_ge(ident_step, 2)
        ones = ctx.enter_context(nc.sbuf_tensor("ones", [P, P], F32))
        ones_set = sem("ones_set")
        with nc.Block() as block:
            @block.vector
            def _(dve):
                dve.memset(ones[:], 1.0).then_inc(ones_set, 1)
                dve.wait_ge(ones_set, 1)
        norm_project_prepare(nc, ident, r8, a, d)
        logits = ctx.enter_context(nc.sbuf_tensor("logits", [P, NT, NEG + NE], F32))
        trunk = ctx.enter_context(ExitStack())
        srs = trunk.enter_context(nc.sbuf_tensor("ssm_rstd", [P, NT], F32))
        with nc.sbuf_tensor("u_tok", [P, 2, CH, SW], F32) as U:
            s5_groups(nc, ident, r8, U, a, d)
            s5_gate(nc, ident, ones, U, srs, a, d)
        with nc.sbuf_tensor("attn_T", [P, HEADS, SEQ], F32) as oT, nc.sbuf_tensor("w_out_first", [P, KT, BANK], F32) as wo:
            attention(nc, ident, oT, wo, a, d)
            out_projection(nc, ident, oT, wo, srs, logits, a, d)
        trunk.close()
        gates = ctx.enter_context(nc.sbuf_tensor("gates", [P, 2, NT], F32))
        dest = ctx.enter_context(nc.sbuf_tensor("dest", [P, 2, NT], I32))
        ids = ctx.enter_context(nc.sbuf_tensor("slot_ids", [P, NBLK + 2], I32))
        meta = ctx.enter_context(nc.sbuf_tensor("block_meta", [P, META], I32))
        route(nc, ident, ones, logits, gates, dest, ids, meta, d)
        experts(nc, ident, ones, ids, meta, a, d)
        combine(nc, gates, dest, a, d, out)



_INS = [
    'x', 'norm_attn', 'w_in', 'lambda_q1', 'lambda_k1', 'lambda_q2', 'lambda_k2', 'attn_subln',
    'ssm_lam_re', 'ssm_lam_im', 'ssm_log_dt', 'ssm_b_re', 'ssm_b_im', 'ssm_c_re', 'ssm_c_im', 'ssm_d',
    'w_glu', 'b_glu', 'ssm_norm', 'w_out', 'norm_moe', 'w_router_group', 'b_router_group', 'w_router_expert',
    'b_router_expert', 'w_gate', 'w_up', 'w_down', 'norm_final',
]
_OUTS = [((1, 2048, 1024), 'float32')]


def kernel(**inputs):
    import numpy as _np
    import concourse.bacc as _bacc
    from concourse import mybir as _mybir
    from concourse.bass_utils import run_bass_kernel_spmd as _run

    nc = _bacc.Bacc("TRN2", target_bir_lowering=False, num_devices=1)
    arrays, aps = {}, {}
    for name in _INS:
        v = _np.ascontiguousarray(inputs[name])
        arrays[f"in_{name}_dram"] = v
        aps[name] = nc.dram_tensor(f"in_{name}_dram", v.shape, _mybir.dt.from_np(v.dtype), kind="ExternalInput").ap()
    shape, dtype = _OUTS[0]
    out = nc.dram_tensor("out_0_dram", shape, _mybir.dt.from_np(_np.dtype(dtype)), kind="ExternalOutput").ap()
    hybrid_layer(nc, aps, out)
    r = _run(nc, [arrays], core_ids=[0])
    return r.results[0]["out_0_dram"]
```
